# Optimizing a Trainium2 kernel written in Bass

```python
import jax, jax.numpy as jnp
from jax import lax
import numpy as np

D_MODEL = 1024
BATCH = 1
SEQ = 1024
DEPTH = 1

D_MIX = D_MODEL
FOX_HEADS = 6
FOX_HEAD_DIM = 64
FOX_WIDTH = FOX_HEADS * FOX_HEAD_DIM
Q_BLOCK = 128
FOX_F_BIAS_INIT = 2.0
S5_CH_PER_GROUP = 16
S5_GROUPS = 16
S5_WIDTH = S5_GROUPS * S5_CH_PER_GROUP
S5_STATE = 64
S5_DT_MIN = 0.001
S5_DT_MAX = 0.1
HGRN_HEADS = 6
HGRN_KEY_DIM = 64
HGRN_VAL_DIM = 64
HGRN_WIDTH = HGRN_HEADS * HGRN_VAL_DIM
HGRN_CHUNK = 64
N_EXPERTS = 16
N_EXPERT_GROUPS = 4
EXPERTS_PER_GROUP = N_EXPERTS // N_EXPERT_GROUPS
TOP_K = 2
D_FF_EXPERT = 256
EPS = 1e-6

IN_SPLITS = (FOX_WIDTH, FOX_WIDTH, FOX_WIDTH, FOX_HEADS, S5_WIDTH, HGRN_WIDTH, HGRN_WIDTH, HGRN_WIDTH, HGRN_WIDTH)
N_IN = sum(IN_SPLITS)
IN_OFFSETS = tuple(int(v) for v in np.cumsum(IN_SPLITS)[:-1])

kernel_name = "hybrid_fox_s5_hgrn2_moe_adaln"

F32 = jnp.float32

def rms_norm(x, w):
    x32 = x.astype(F32)
    y = x32 * lax.rsqrt(jnp.mean(x32 * x32, axis=-1, keepdims=True) + EPS)
    return (y * w.astype(F32)).astype(x.dtype)

def fox_attention(q, k, v, log_f):
    bsz, seq = q.shape[0], q.shape[1]
    q = jnp.transpose(q, (0, 2, 1, 3)).astype(F32)
    k = jnp.transpose(k, (0, 2, 1, 3)).astype(F32)
    v = jnp.transpose(v, (0, 2, 1, 3)).astype(F32)
    cum = jnp.transpose(jnp.cumsum(log_f, axis=1), (0, 2, 1))
    scale = FOX_HEAD_DIM ** -0.5
    outs = []
    for blk in range(seq // Q_BLOCK):
        lo, hi = blk * Q_BLOCK, (blk + 1) * Q_BLOCK
        logits = jnp.einsum('bhqd,bhkd->bhqk', q[:, :, lo:hi], k[:, :, :hi]) * scale
        logits = logits + cum[:, :, lo:hi, None] - cum[:, :, None, :hi]
        causal = (lo + jnp.arange(Q_BLOCK))[:, None] >= jnp.arange(hi)[None, :]
        probs = jax.nn.softmax(jnp.where(causal, logits, -jnp.inf), axis=-1)
        outs.append(jnp.einsum('bhqk,bhkd->bhqd', probs, v[:, :, :hi]))
    o = jnp.concatenate(outs, axis=2)
    return jnp.transpose(o, (0, 2, 1, 3)).reshape(bsz, seq, FOX_WIDTH)

def _diag_linear_combine(e1, e2):
    a1, b1 = e1
    a2, b2 = e2
    return a1 * a2, a2 * b1 + b2

def s5_mixer(u, a_re, a_im, b_re, b_im, c_re, c_im, d, log_dt, glu_w, glu_b):
    bsz, seq = u.shape[0], u.shape[1]
    u32 = u.astype(F32).reshape(bsz, seq, S5_GROUPS, S5_CH_PER_GROUP)
    lam = lax.complex(a_re.astype(F32), a_im.astype(F32))
    dt = jnp.exp(log_dt.astype(F32))[:, None]
    a_bar = jnp.exp(lam * dt)
    b_bar = ((a_bar - 1.0) / lam)[..., None] * lax.complex(b_re.astype(F32), b_im.astype(F32))
    bu = jnp.einsum('btgc,gpc->btgp', u32.astype(jnp.complex64), b_bar)
    a_seq = jnp.broadcast_to(a_bar, bu.shape)
    _, states = lax.associative_scan(_diag_linear_combine, (a_seq, bu), axis=1)
    c_mat = lax.complex(c_re.astype(F32), c_im.astype(F32))
    y = jnp.real(jnp.einsum('btgp,gcp->btgc', states, c_mat)) + d.astype(F32) * u32
    y = jax.nn.gelu(y.reshape(bsz, seq, S5_WIDTH))
    gate = jax.nn.sigmoid(y @ glu_w.astype(F32) + glu_b.astype(F32))
    return (y * gate).astype(u.dtype)

def _hgrn2_chunk(state, chunk):
    q, k, v, log_f = chunk
    n = q.shape[2]
    b = jnp.cumsum(log_f, axis=2)
    causal = jnp.tril(jnp.ones((n, n), dtype=bool))
    diff = b[:, :, :, None, :] - b[:, :, None, :, :]
    decay = jnp.exp(jnp.where(causal[:, :, None], diff, -jnp.inf))
    scores = jnp.einsum('bhtd,bhsd,bhtsd->bhts', q, k, decay)
    o = jnp.einsum('bhts,bhsv->bhtv', scores, v) + jnp.einsum('bhtd,bhdv->bhtv', q * jnp.exp(b), state)
    b_last = b[:, :, -1:, :]
    new_state = jnp.exp(b_last[:, :, 0, :])[..., None] * state + jnp.einsum('bhsd,bhsv->bhdv', k * jnp.exp(b_last - b), v)
    return new_state, o

def hgrn2_mixer(q, f_logit, inp, g, lower_bound, norm_w):
    bsz, seq = q.shape[0], q.shape[1]
    n_chunks = seq // HGRN_CHUNK
    z = f_logit.astype(F32)
    lb = lower_bound.astype(F32)
    log_f = jnp.logaddexp(jnp.log(lb), jnp.log1p(-lb) + jax.nn.log_sigmoid(z))
    key = (1.0 - lb) * jax.nn.sigmoid(-z)
    qf = jax.nn.silu(q.astype(F32))

    def to_chunks(t, dim):
        t = t.reshape(bsz, n_chunks, HGRN_CHUNK, HGRN_HEADS, dim)
        return jnp.transpose(t, (1, 0, 3, 2, 4))

    xs = (to_chunks(qf, HGRN_KEY_DIM), to_chunks(key, HGRN_KEY_DIM),
          to_chunks(inp.astype(F32), HGRN_VAL_DIM), to_chunks(log_f, HGRN_KEY_DIM))
    s0 = jnp.zeros((bsz, HGRN_HEADS, HGRN_KEY_DIM, HGRN_VAL_DIM), F32)
    _, o = lax.scan(_hgrn2_chunk, s0, xs)
    o = jnp.transpose(o, (1, 0, 3, 2, 4)).reshape(bsz, seq, HGRN_HEADS, HGRN_VAL_DIM)
    o = rms_norm(o, norm_w).reshape(bsz, seq, HGRN_WIDTH) * jax.nn.silu(g.astype(F32))
    return o.astype(q.dtype)

def moe_ffn(h, router_w, router_b, w_gate, w_up, w_down):
    bsz, seq, d = h.shape
    t = h.reshape(-1, d)
    logits = (t @ router_w + router_b).astype(F32)
    probs = jax.nn.softmax(logits, axis=-1)
    grouped = probs.reshape(-1, N_EXPERT_GROUPS, EXPERTS_PER_GROUP)
    group_score = lax.top_k(grouped, TOP_K)[0].sum(-1)
    best = jnp.argmax(group_score, axis=-1)
    in_group = jnp.take_along_axis(grouped, best[:, None, None], axis=1)[:, 0]
    top_w, top_i = lax.top_k(in_group, TOP_K)
    top_w = top_w / jnp.sum(top_w, axis=-1, keepdims=True)
    idx = best[:, None] * EXPERTS_PER_GROUP + top_i
    combine = jnp.sum(jax.nn.one_hot(idx, N_EXPERTS, dtype=F32) * top_w[..., None], axis=1)
    y = jnp.zeros(t.shape, F32)
    for e in range(N_EXPERTS):
        hid = jax.nn.silu(t @ w_gate[e]) * (t @ w_up[e])
        y = y + combine[:, e:e + 1] * (hid @ w_down[e]).astype(F32)
    return y.reshape(bsz, seq, d).astype(h.dtype)

def setup_inputs(seed: int = 0) -> dict:
    key = jax.random.key(seed)
    ks = jax.random.split(key, 32)

    def nrm(k, shape, scale):
        return scale * jax.random.normal(k, shape, F32)

    n_idx = jnp.arange(S5_STATE, dtype=F32)
    return {
        "x": nrm(ks[0], (BATCH, SEQ, D_MODEL), 1.0),
        "c": nrm(ks[1], (BATCH, D_MODEL), 1.0),
        "ada_w": nrm(ks[2], (DEPTH, D_MODEL, 6 * D_MODEL), 0.3 * D_MODEL ** -0.5),
        "ada_b": nrm(ks[3], (DEPTH, 6 * D_MODEL), 0.01),
        "norm_mix_w": 1.0 + nrm(ks[4], (DEPTH, D_MODEL), 0.02),
        "norm_ffn_w": 1.0 + nrm(ks[5], (DEPTH, D_MODEL), 0.02),
        "w_in": nrm(ks[6], (DEPTH, D_MODEL, N_IN), D_MODEL ** -0.5),
        "fox_f_bias": FOX_F_BIAS_INIT + nrm(ks[7], (DEPTH, FOX_HEADS), 0.1),
        "s5_a_re": -0.5 + nrm(ks[8], (DEPTH, S5_GROUPS, S5_STATE), 0.01),
        "s5_a_im": jnp.broadcast_to(jnp.pi * n_idx, (DEPTH, S5_GROUPS, S5_STATE)) + nrm(ks[9], (DEPTH, S5_GROUPS, S5_STATE), 0.01),
        "s5_b_re": nrm(ks[10], (DEPTH, S5_GROUPS, S5_STATE, S5_CH_PER_GROUP), (2 * S5_CH_PER_GROUP) ** -0.5),
        "s5_b_im": nrm(ks[11], (DEPTH, S5_GROUPS, S5_STATE, S5_CH_PER_GROUP), (2 * S5_CH_PER_GROUP) ** -0.5),
        "s5_c_re": nrm(ks[12], (DEPTH, S5_GROUPS, S5_CH_PER_GROUP, S5_STATE), 0.5),
        "s5_c_im": nrm(ks[13], (DEPTH, S5_GROUPS, S5_CH_PER_GROUP, S5_STATE), 0.5),
        "s5_d": nrm(ks[14], (DEPTH, S5_GROUPS, S5_CH_PER_GROUP), 1.0),
        "s5_log_dt": jax.random.uniform(ks[15], (DEPTH, S5_GROUPS), F32, float(np.log(S5_DT_MIN)), float(np.log(S5_DT_MAX))),
        "s5_glu_w": nrm(ks[16], (DEPTH, S5_WIDTH, S5_WIDTH), S5_WIDTH ** -0.5),
        "s5_glu_b": nrm(ks[17], (DEPTH, S5_WIDTH), 0.01),
        "hgrn_lb_logits": nrm(ks[18], (DEPTH, HGRN_WIDTH), 0.1),
        "hgrn_norm_w": 1.0 + nrm(ks[19], (DEPTH, HGRN_VAL_DIM), 0.02),
        "branch_norm_fox": 1.0 + nrm(ks[20], (DEPTH, FOX_WIDTH), 0.02),
        "branch_norm_s5": 1.0 + nrm(ks[21], (DEPTH, S5_WIDTH), 0.02),
        "w_out": nrm(ks[22], (DEPTH, D_MIX, D_MODEL), D_MIX ** -0.5),
        "router_w": nrm(ks[23], (D_MODEL, N_EXPERTS), D_MODEL ** -0.5),
        "router_b": nrm(ks[24], (N_EXPERTS,), 0.01),
        "moe_w_gate": nrm(ks[25], (DEPTH, N_EXPERTS, D_MODEL, D_FF_EXPERT), D_MODEL ** -0.5),
        "moe_w_up": nrm(ks[26], (DEPTH, N_EXPERTS, D_MODEL, D_FF_EXPERT), D_MODEL ** -0.5),
        "moe_w_down": nrm(ks[27], (DEPTH, N_EXPERTS, D_FF_EXPERT, D_MODEL), D_FF_EXPERT ** -0.5),
        "final_norm_w": 1.0 + nrm(ks[28], (D_MODEL,), 0.02),
    }

def reference(x, c, ada_w, ada_b, norm_mix_w, norm_ffn_w, w_in, fox_f_bias,
              s5_a_re, s5_a_im, s5_b_re, s5_b_im, s5_c_re, s5_c_im, s5_d, s5_log_dt,
              s5_glu_w, s5_glu_b, hgrn_lb_logits, hgrn_norm_w, branch_norm_fox, branch_norm_s5,
              w_out, router_w, router_b, moe_w_gate, moe_w_up, moe_w_down, final_norm_w):
    bsz, seq, _ = x.shape
    lb_cum = jnp.cumsum(jax.nn.softmax(hgrn_lb_logits.astype(F32), axis=0), axis=0)
    lower_bounds = lb_cum - lb_cum[0:1]
    c_act = jax.nn.silu(c)
    for layer in range(DEPTH):
        mod = c_act @ ada_w[layer] + ada_b[layer]
        sh_m, sc_m, g_m, sh_f, sc_f, g_f = [m[:, None, :] for m in jnp.split(mod, 6, axis=-1)]
        h = rms_norm(x, norm_mix_w[layer]) * (1 + sc_m) + sh_m
        z = h @ w_in[layer]
        fq, fk, fv, ff, su, hq, hf, hi, hg = jnp.split(z, IN_OFFSETS, axis=-1)
        heads4 = (bsz, seq, FOX_HEADS, FOX_HEAD_DIM)
        fox_log_f = jax.nn.log_sigmoid(ff.astype(F32) + fox_f_bias[layer].astype(F32))
        o_fox = fox_attention(fq.reshape(heads4), fk.reshape(heads4), fv.reshape(heads4), fox_log_f).astype(x.dtype)
        o_fox = rms_norm(o_fox, branch_norm_fox[layer])
        o_s5 = s5_mixer(su, s5_a_re[layer], s5_a_im[layer], s5_b_re[layer], s5_b_im[layer],
                        s5_c_re[layer], s5_c_im[layer], s5_d[layer], s5_log_dt[layer],
                        s5_glu_w[layer], s5_glu_b[layer]).astype(x.dtype)
        o_s5 = rms_norm(o_s5, branch_norm_s5[layer])
        o_hgrn = hgrn2_mixer(hq, hf, hi, hg, lower_bounds[layer], hgrn_norm_w[layer]).astype(x.dtype)
        mix = jnp.concatenate([o_fox, o_s5, o_hgrn], axis=-1) @ w_out[layer]
        x = x + g_m * mix
        h = rms_norm(x, norm_ffn_w[layer]) * (1 + sc_f) + sh_f
        x = x + g_f * moe_ffn(h, router_w, router_b, moe_w_gate[layer], moe_w_up[layer], moe_w_down[layer])
    return rms_norm(x, final_norm_w)


_drawn_inputs = setup_inputs


def setup_inputs(seed=0):
    import zlib

    import numpy as np

    out = dict(_drawn_inputs(seed))
    spreads = {}
    factors = {'ada_b': 3.412,
     'norm_mix_w': 6.957,
     'norm_ffn_w': 4.194,
     'fox_f_bias': 6.228,
     's5_a_re': 64.0,
     's5_glu_b': 28.239,
     'hgrn_norm_w': 8.0,
     'branch_norm_fox': 39.093,
     'branch_norm_s5': 64.0,
     'router_b': 4.045,
     'final_norm_w': 7.507}
    for name, (base, spread) in spreads.items():
        noise = np.random.default_rng([zlib.crc32(name.encode()), seed]).standard_normal(out[name].shape)
        drawn = base * np.exp(spread * noise) if base else spread * noise
        out[name] = __import__('jax').numpy.asarray(drawn.astype(out[name].dtype))
    for name, factor in factors.items():
        out[name] = (out[name] * factor).astype(out[name].dtype)
    return out
```

```python
from contextlib import ExitStack

import numpy as np
import concourse.bass as bass
from concourse import mybir

ALU = mybir.AluOpType
ACT = mybir.ActivationFunctionType
F32 = mybir.dt.float32
I32 = mybir.dt.int32
BF16 = mybir.dt.bfloat16
AX_X = mybir.AxisListType.X

P = 128
D = 1024
T = 1024
KD = D // P
NT = T // P
EPS = 1e-6
FOX_H, FOX_D = 6, 64
FOX_W = FOX_H * FOX_D
S5_G, S5_C, S5_P = 16, 16, 64
S5_W = S5_G * S5_C
S5_M = S5_G // 2
S5_L = 8
S5_J = T // S5_L
HG_H, HG_D = 6, 64
HG_W = HG_H * HG_D
HG_M = HG_W // P
NE, NG, PG = 16, 4, 4
FF = 256
ADA = 6 * D
ADA_N = 512
TILES = (2 * T + NE * (P - 1)) // P
SLOTS = TILES * P
TWO_PI = 6.2831850
ROUND = 12582912.0

O_FQ, O_FK, O_FV = 0, FOX_W, 2 * FOX_W
O_SU = 3 * FOX_W + FOX_H
O_HQ = O_SU + S5_W
O_HF, O_HI, O_HG = O_HQ + HG_W, O_HQ + 2 * HG_W, O_HQ + 3 * HG_W
N_IN = O_HQ + 4 * HG_W
VW = FOX_W + FOX_H

GROUPS = [
    ("su", O_SU, S5_W, True, "dve"),
    ("hq", O_HQ, HG_W, False, "act"),
    ("hi", O_HI, HG_W, True, "dve"),
    ("hg", O_HG, HG_W, True, "act"),
    ("hf", O_HF, HG_W, False, "dve"),
    ("fv", O_FV, VW, True, "dve"),
    ("fq", O_FQ, FOX_W, False, "act"),
    ("fk", O_FK, FOX_W, False, "dve"),
]
UNITS = []
for gi, (_, _, _, tok, _) in enumerate(GROUPS):
    UNITS += [(gi, u) for u in range(NT)] if tok else [(gi, (m, h)) for m in range(3) for h in range(2)]
WIN_BANKS = 4
LEVELS = [64, 32, 16, 8, 4, 2, 1]


def evacuated(engine, u):
    return sum(GROUPS[g][4] == engine for g, _ in UNITS[:u + 1])


STEPS = {
    "pe": "s5_W_tr s5_kern s5_U_tr s5_V_mm s5_y_mm s5_y_tr s5_glu_mm s5_o_tr f_tr count_mm".split(),
    "act": "cact s5_dt s5_gate hk_ready e_b efin e_kb rt_exp".split(),
    "dve": "s5_ph s5_rot s5_BA s5_CA kz_full sssq s5_o qe_ready ke_ready cum_ready rt_sub chosen expert_ready".split(),
    "pool": "mhalf_set list_zero kz_zero rstd_x srstd d_kb w_scaled a2_mul a2_ready tok_ready".split(),
}


def unit_range(name):
    return [u for u, (g, _) in enumerate(UNITS) if GROUPS[g][0] == name]


C_ID, C_ONE, C_LT, C_NEG = 0, P, 2 * P, 3 * P
C_J = 4 * P
C_POW = 5 * P
C_THR = C_POW + 17
C_RANK = C_THR + 8
C_TOK = C_RANK + 4
C_F = C_TOK + NT
S5_PAR = 3 * S5_M + S5_G + 4 * S5_M * S5_C


def shape_constants():
    p = np.arange(P)
    c = np.zeros((P, C_F), np.float32)
    c[:, C_ID:C_ID + P] = np.eye(P)
    c[:, C_ONE:C_ONE + P] = 1.0
    c[:, C_LT:C_LT + P] = p[:, None] < p[None, :]
    c[:, C_NEG:C_NEG + P] = np.where(p[None, :] > p[:, None], -1e30, 0.0)
    c[:, C_J:C_J + P] = p[None, :]
    c[:, C_POW:C_POW + 17] = np.r_[np.arange(9), np.arange(7, -1, -1)]
    c[:, C_THR:C_THR + 8] = 128.0 * np.arange(8)
    c[:, C_RANK:C_RANK + 4] = [3, 2, 1, 0]
    c[:, C_TOK:C_TOK + NT] = p[:, None] + P * np.arange(NT)
    m = np.zeros((P, 1 + len(LEVELS), P), np.int32)
    m[:, 0] = np.eye(P)
    s, t = p[:, None], p[None, :]
    for n, half in enumerate(LEVELS):
        m[:, 1 + n] = (s // (2 * half) == t // (2 * half)) & (s % (2 * half) < half) & (t % (2 * half) >= half)
    return c, m.reshape(P, -1)


def hybrid_trunk_layer(nc, A, out):
    ctx = ExitStack()
    with ctx:
        def sb(name, cols, dt=F32):
            return ctx.enter_context(nc.sbuf_tensor(name, [P, cols], dt))

        sems = {}

        def sem(name):
            if name not in sems:
                sems[name] = ctx.enter_context(nc.semaphore(name))
            return sems[name]

        def step(name):
            return sem(next(f"{e}_step" for e in STEPS if name in STEPS[e]))

        def nth(name):
            return next(STEPS[e].index(name) + 1 for e in STEPS if name in STEPS[e])

        def dram(name, shape, dt=F32):
            return nc.dram_tensor(name, shape, dt, kind="Internal").ap()

        mod_d = dram("mod_d", (6, D))
        kern_d = dram("kern_d", (S5_C, S5_G, 2 * P))
        h2_d = dram("h2_d", (T, D))
        list_d = dram("list_d", (SLOTS, 1), I32)
        y_d = dram("y_d", (SLOTS, D))

        psum = ctx.enter_context(nc.psum_tensor("psum", [P, 4096], F32))

        def bank(b, n=1):
            return psum[:, 512 * b:512 * (b + n)]

        cst = sb("cst", C_F)
        lmask = sb("lmask", (1 + len(LEVELS)) * P, I32)
        ident, ones = cst[:, C_ID:C_ID + P], cst[:, C_ONE:C_ONE + P]
        masks = lmask[:].rearrange("p (l t) -> p l t", t=P)
        small = sb("small", 780)
        ident16, neg16 = sb("ident16", P, BF16), sb("neg16", P, BF16)
        at = [0]

        def little(n, dt=F32):
            v = small[:, at[0]:at[0] + n]
            at[0] += n
            return v if dt == F32 else v.bitcast(dt)

        cact = little(KD)
        ssq, rstd = little(NT), little(NT)
        mhalf = little(NT * HG_H)
        late = little(FOX_H + KD + KD * NE + NE)
        fbias = late[:, 0:FOX_H]
        wrow = late[:, FOX_H:FOX_H + KD]
        router_w = late[:, FOX_H + KD:FOX_H + KD + KD * NE].rearrange("p (k e) -> p k e", e=NE)
        router_b = late[0:1, FOX_H + KD + KD * NE:]
        hg_ss, hg_r, rowsum = little(NT * HG_H), little(NT * HG_H), little(NT * FOX_H)
        negmax, rinv = hg_ss, hg_r
        fssq, frstd, sssq, srstd = little(NT), little(NT), little(NT), little(NT)
        efin = little(HG_M * NT)
        flog, fln = little(NT * FOX_H), little(NT * FOX_H)

        def cut(region, start, *shape):
            n = int(np.prod(shape))
            v = region[:, start:start + n]
            if len(shape) == 1:
                return v
            names = "abcd"[:len(shape)]
            return v.rearrange(f"p ({' '.join(names)}) -> p {' '.join(names)}",
                               **{k: s for k, s in zip(names[1:], shape[1:])})

        ra = sb("region_a", 12288)
        rb = sb("region_b", 8192)
        rc = sb("region_c", 8192)
        rd = sb("region_d", 15360)
        re_ = sb("region_e", 6512)

        hT = cut(rb, 0, KD, T)
        ada_ring = [cut(rc, 4096 * i, KD, ADA_N) for i in range(2)]
        win_ring = [cut(rc, 4096 * i, KD, 512) for i in range(2)]
        x_sb = cut(rd, 0, NT, D)
        mod_row = rd[0:1, 8192:8192 + ADA]
        a1b, b1b, nmw = cut(ra, 0, D), cut(ra, 1024, D), cut(ra, 2048, D)

        hq, hb, hk = cut(rd, 0, HG_M, T), cut(rd, 3072, HG_M, T), cut(rd, 6144, HG_M, T)
        hv, hgate = cut(rd, 9216, NT, HG_W), cut(rd, 12288, NT, HG_W)
        fv = cut(re_, 0, NT, VW)
        cS5 = cut(re_, 3120, 2, T)
        hg_tmp = cut(re_, 5168, T)

        s5_W = cut(ra, 3072, S5_M, 2, P)
        s5_CA = cut(ra, 5120, 2, S5_M, 9, S5_C)
        s5_T = cut(ra, 7424, S5_G, P)
        s5_cos, s5_sin = cut(ra, 9472, S5_M * S5_J), cut(ra, 10496, S5_M * S5_J)
        glu_w = cut(ra, 11520, 2, S5_W)
        glu_b = ra[0:1, 12032:12288]
        s5_R = cut(re_, 5168, S5_M * S5_J)
        kz = rb[0:S5_C, 0:S5_G * 2 * P].rearrange("c (g x) -> c g x", g=S5_G)
        s5_BA = cut(rb, 4096, 2, S5_M, S5_L, S5_C)
        s5_par = rb[:, 6144:6144 + S5_PAR]
        are, aim, dt = [s5_par[:, 8 * i:8 * i + 8] for i in range(3)]
        s5_D = s5_par[0:S5_C, 24:40]
        s5_B = cut(s5_par, 40, 2, S5_M, S5_C)
        s5_Ct = cut(s5_par, 296, 2, S5_M, S5_C)
        s5_bb = cut(rb, 6704, 2, S5_M, S5_C)
        p_mag, p_re, p_im, p_tmp = [cut(rb, 6960 + 136 * i, S5_M, 17) for i in range(4)]
        lr, th, ph8, den, wr, wi, am1, u0, u1 = [cut(re_, 8 * i, S5_M) for i in range(9)]
        s5_tab = [ra[:, 7424:8448], ra[:, 8448:9472]]
        s5_Z = cut(ra, 0, S5_G, S5_L, S5_C)
        s5_V = cut(ra, 0, 2, S5_M * S5_J)
        s5_yT = cut(ra, 0, 2, S5_L, S5_J)
        s5_U = cut(rd, 3072, S5_G, S5_J)
        s5_X = [cut(rd, 5120, S5_M, S5_J), cut(rd, 8192, S5_M, S5_J)]
        s5_t = [cut(rd, 6144, S5_M * S5_J), cut(rd, 7168, S5_M * S5_J)]
        s5_y = cut(rd, 6144, S5_L, S5_W)
        s5_gate = cut(ra, 9472, S5_L, S5_W)
        s5_sq = cut(ra, 7424, S5_L, S5_W)
        qaug, kaug = cut(ra, 0, FOX_H, T), cut(ra, 6144, FOX_H, T)

        qe, ke = cut(rb, 0, HG_M, T), cut(rb, 3072, HG_M, T)
        keT = [cut(rb, 6144 + 384 * n, HG_W) if n < 5 else cut(rc, 6144 + 384 * (n - 5), HG_W) for n in range(NT)]
        lev = [cut(rc, 1536 * i, HG_M, 512) for i in range(2)]
        sT = cut(rc, 3072, HG_H, 4, P)
        hg_S = cut(re_, 5168, NT - 1, HG_M * HG_D)
        hg_o = cut(rc, 0, 4 * HG_H, HG_D)
        hg_sq = cut(rc, 1536, 4 * HG_H, HG_D)
        cHg = cut(rd, 3072, HG_M, T)
        n_lev = len(LEVELS)
        prob = [cut(rd, 6144 + T * i, T) for i in range(2)]
        probT = [cut(rd, 8192 + T * i, NT, P) for i in range(2)]
        cum, ncum = rd[0:FOX_H, 10240:11264], rd[0:FOX_H, 11264:12288]
        fo = [cut(rd, 12288 + FOX_W * i, FOX_W) for i in range(2)]
        fsq = cut(rd, 13056, FOX_W)
        cFox = cut(rd, 0, 3, T)
        units = [(i, h) for i in range(NT) for h in range(FOX_H)]
        x2 = cut(rb, 0, NT, D)
        w_out = cut(rc, 0, KD, D)
        gmb, b2b, a2b, nfw = cut(rd, 10240, D), cut(rd, 11264, D), cut(rd, 13440, D), cut(re_, 5168, D)
        mix_t = [cut(ra, D * i, D) for i in range(2)]
        h2 = [cut(ra, 2048 + D * i, D) for i in range(2)]
        h2T = [cut(ra, 4096 + D * i, KD, P) for i in range(2)]
        sq2 = cut(ra, 6144, D)
        ssq2, rstd2, ssq3, rstd3 = little(NT), little(NT), little(NT), little(NT)
        branch = [cFox[:, 0], cFox[:, 1], cFox[:, 2], cS5[:, 0], cS5[:, 1], cHg[:, 0], cHg[:, 1], cHg[:, 2]]
        rt = [rd[:, 6144 + P * i:6144 + P * (i + 1)] for i in range(12)]
        rs_ = [rd[:, 7680 + 32 * i:7680 + 32 * (i + 1)] for i in range(12)]
        thr = cut(rd, 8192, NE, NT)
        til = cut(rd, 8320, 32, NE)
        slot_a, slot_b = little(NT, I32), little(NT, I32)
        wgt_a, wgt_b = little(NT), little(NT)
        tok_i, tok_l = little(NT, I32), little(TILES, I32)
        expert_i = little(32, I32)
        wgu = [cut(r_, o, KD, 2 * FF) for r_, o in ((ra, 0), (ra, 6144), (rd, 0), (rd, 6144))]
        wdn = [cut(r_, o, 2, D) for r_, o in ((ra, 4096), (ra, 10240), (rd, 4096), (rd, 10240))]
        rows = [cut(rc, D * i, D) for i in range(4)]
        rowT = [cut(rc, 4096 + D * i, KD, P) for i in range(2)]
        answer = [cut(rc, 6144 + D * i, D) for i in range(2)]
        silu = [cut(rd, 12288 + FF * i, FF) for i in range(2)]
        hid = [cut(rd, 12800 + FF * i, FF) for i in range(2)]
        hidT = [cut(rd, 13312 + FF * i, 2, P) for i in range(2)]
        gfb, fnw = cut(re_, 0, D), cut(re_, D, D)
        NY = 6
        y_a, y_b = [cut(ra, 2 * D * i, D) for i in range(NY)], [cut(ra, 2 * D * i + D, D) for i in range(NY)]
        fin = [cut(rd, D * i, D) for i in range(2)]
        sq3 = cut(rd, 2 * D, D)

        def each_tile(eng, body):
            for t in range(4):
                body(t, t, 0)
            with eng.Fori(1, TILES // 4) as i:
                for j in range(4):
                    body(4 * i + j, j, i)
            for t in range(TILES // 4 * 4, TILES):
                body(t, t % 4, t // 4)

        def b3(v, n):
            return v.unsqueeze(2).to_broadcast([v.shape[0], v.shape[1], n])

        block = ctx.enter_context(nc.Block())

        @block.sync
        def _(sp):
            for n in range(ADA // ADA_N):
                if n >= 2:
                    sp.wait_ge(sem("ada_mm"), n - 1)
                sp.dma_start(ada_ring[n % 2], A["ada_w"][n]).then_inc(sem(f"ada_in{n % 2}"), 16)
                if n == 0:
                    sp.dma_start(mod_row, A["ada_b"]).then_inc(sem("ada_b_in"), 16)
                if n == 1:
                    sp.dma_start(x_sb, A["x"][0].rearrange("(i p) d -> p i d", p=P)).then_inc(sem("x_in"), 16)
            for g, (name, o, w, tok, _) in enumerate(GROUPS):
                if g < 2:
                    sp.wait_ge(sem("ada_mm"), ADA // ADA_N - 1 + g)
                else:
                    sp.wait_ge(sem("win_mm"), unit_range(GROUPS[g - 2][0])[-1] + 1)
                sp.dma_start(win_ring[g % 2][:, :, 0:w], A["w_in"][:, :, o:o + w]).then_inc(sem(f"win_in{g % 2}"), 16)

            sp.wait_ge(sem("hg_gated"), 2)
            sp.dma_start(rc[:], A["w_out"]).then_inc(sem("w_out_in"), 16)
            sp.dma_start(x2, A["x"][0].rearrange("(i p) d -> p i d", p=P)).then_inc(sem("x2_in"), 16)
            for i in range(NT):
                sp.wait_ge(sem("h2_ready"), i + 1)
                sp.dma_start(h2_d[i * P:(i + 1) * P], h2[i % 2]).then_inc(sem(f"h2_out{i % 2}"), 16)

            sp.wait_ge(step("expert_ready"), nth("expert_ready"))

            def load(t, j, r):
                e = sp.value_load(expert_i[0:1, bass.ds(t, 1)], min_val=0, max_val=NE - 1)
                if not (isinstance(r, int) and r == 0):
                    sp.wait_ge(sem("moe_gu"), 4 * r + j - 3)
                sp.dma_start(wgu[j], A["gate_up"][bass.ds(e, 1)].rearrange("o p k n -> (o p) k n")).then_inc(sem(f"gu_in{j}"), 16)
                if not (isinstance(r, int) and r == 0):
                    sp.wait_ge(sem("moe_dn"), 4 * r + j - 3)
                sp.dma_start(wdn[j], A["down"][bass.ds(e, 1)].rearrange("o p k n -> (o p) k n")).then_inc(sem(f"dn_in{j}"), 16)

            each_tile(sp, load)
            for i in range(NT):
                sp.wait_ge(sem("fin_ready"), i + 1)
                sp.dma_start(out[0, i * P:(i + 1) * P], fin[i % 2]).then_inc(sem(f"out{i % 2}"), 16)
            for i in range(2):
                sp.wait_ge(sem(f"out{i}"), 16 * NT // 2)

        @block.gpsimd
        def _(pool):
            pool.memset(mhalf, -0.5).then_inc(step("mhalf_set"), 1)
            pool.wait_ge(step("mhalf_set"), nth("mhalf_set"))
            pool.memset(tok_l, 0).then_inc(step("list_zero"), 1)
            pool.dma_start(cact, A["c_col"]).then_inc(sem("c_in"), 16)
            pool.dma_start(s5_par, A["s5_par"]).then_inc(sem("s5_in"), 16)
            pool.dma_start(cst[:], A["cst"]).then_inc(sem("const_in"), 16)
            pool.dma_start(lmask[:], A["lmask"]).then_inc(sem("const_in"), 16)
            pool.dma_start(late, A["late"]).then_inc(sem("late_in"), 16)
            pool.memset(kz, 0.0).then_inc(step("kz_zero"), 1)
            pool.dma_start(nmw, A["norms"][0:1].to_broadcast([P, D])).then_inc(sem("nmw_in"), 16)
            pool.wait_ge(sem("ssq_x"), NT)
            pool.tensor_scalar(rstd, ssq, 1.0 / D, EPS, ALU.mult, ALU.add).then_inc(sem("pool_rs"), 1)
            pool.wait_ge(sem("pool_rs"), 1)
            pool.tensor_tensor(rstd, rstd, mhalf[:, 0:NT], ALU.pow).then_inc(step("rstd_x"), 1)
            pool.wait_ge(sem("mod_row"), 4)
            pool.dma_start(mod_d[0:2].rearrange("(o a) d -> o (a d)", o=1), mod_row[:, 0:2 * D]).then_inc(sem("mod_out"), 16)
            pool.wait_ge(sem("mod_out"), 16)
            pool.dma_start(b1b, mod_d[0:1].to_broadcast([P, D])).then_inc(sem("mod1_in"), 16)
            pool.dma_start(a1b, mod_d[1:2].to_broadcast([P, D])).then_inc(sem("mod1_in"), 16)
            pool.wait_ge(sem("mod1_in"), 32)
            for i in range(NT):
                pool.wait_ge(sem("h_mul"), i + 1)
                pool.tensor_tensor(x_sb[:, i], x_sb[:, i], b1b, ALU.add).then_inc(sem("h_add"), 1)
            pool.wait_ge(step("kz_full"), nth("kz_full"))
            pool.dma_start(kern_d, kz).then_inc(sem("kern_out"), 16)
            pool.wait_ge(sem("kern_out"), 16)
            for st in range(S5_L):
                pool.dma_start(s5_T[16 * st:16 * st + 16], kern_d[:, :, P - 16 * st:2 * P - 16 * st]).then_inc(sem("s5_T_in"), 16)
            pool.dma_start(ra[:, 11520:12288], A["glu"]).then_inc(sem("glu_in"), 16)
            pool.wait_ge(sem("mod_row"), 12)
            pool.dma_start(mod_d[2:6].rearrange("(o a) d -> o (a d)", o=1), mod_row[:, 2 * D:]).then_inc(sem("mod_out"), 16)
            pool.wait_ge(step("sssq"), nth("sssq"))
            pool.tensor_scalar(srstd, sssq, 1.0 / S5_W, EPS, ALU.mult, ALU.add).then_inc(sem("pool_rs"), 1)
            pool.wait_ge(sem("pool_rs"), 2)
            pool.tensor_tensor(srstd, srstd, mhalf[:, 0:NT], ALU.pow).then_inc(step("srstd"), 1)
            pool.wait_ge(sem("s5_done"), 4)
            pool.wait_ge(sem("win_mm"), len(UNITS))
            for n, w in enumerate((qaug, kaug)):
                pool.memset(w[64:66], 1.0).then_inc(sem("aug_ones"), 1)
                pool.wait_ge(sem("aug_ones"), n + 1)
            pool.wait_ge(sem("hb_ready"), HG_M * NT)
            chunks = lambda v: v.rearrange("p m (n t) -> p m n t", t=P)
            pool.tensor_tensor(chunks(ke), chunks(hb)[:, :, :, P - 1:P].to_broadcast([P, HG_M, NT, P]), chunks(hb), ALU.subtract).then_inc(step("d_kb"), 1)

            def distances(c):
                rnd, l = c // n_lev, c % n_lev + 1
                v = hb[:, :, 512 * rnd:512 * rnd + 512].rearrange("p m (b two x) -> p m b two x", two=2, x=LEVELS[l - 1])
                o = lev[c % 2].rearrange("p m (b two x) -> p m b two x", two=2, x=LEVELS[l - 1])
                mid = v[:, :, :, 0, LEVELS[l - 1] - 1:LEVELS[l - 1]].to_broadcast([P, HG_M, 256 // LEVELS[l - 1], LEVELS[l - 1]])
                pool.tensor_tensor(o[:, :, :, 0], mid, v[:, :, :, 0], ALU.subtract).then_inc(sem("lev_d0"), 1)
                pool.wait_ge(sem("lev_d0"), c + 1)
                pool.tensor_tensor(o[:, :, :, 1], v[:, :, :, 1], mid, ALU.subtract).then_inc(sem("lev_d"), 1)

            def keys_in(c):
                rnd, l = c // n_lev, c % n_lev + 1
                o = lev[c % 2].rearrange("p m (b two x) -> p m b two x", two=2, x=LEVELS[l - 1])[:, :, :, 0]
                v = hk[:, :, 512 * rnd:512 * rnd + 512].rearrange("p m (b two x) -> p m b two x", two=2, x=LEVELS[l - 1])[:, :, :, 0]
                pool.wait_ge(sem("lev_exp"), c + 1)
                pool.tensor_tensor(o, o, v, ALU.mult).then_inc(sem("lev_k"), 1)

            for rnd in range(2):
                if rnd:
                    pool.wait_ge(sem("hg_gated"), rnd)
                distances(rnd * n_lev)
                for c in range(rnd * n_lev, (rnd + 1) * n_lev):
                    if c + 1 < (rnd + 1) * n_lev:
                        if c % n_lev >= 1:
                            pool.wait_ge(sem("hg_mm"), (rnd * (1 + n_lev) + c % n_lev + 1) * HG_H)
                        distances(c + 1)
                    keys_in(c)
                v = slice(24 * rnd, 24 * rnd + 24)
                pool.wait_ge(sem("hg_ss"), rnd + 1)
                pool.tensor_scalar(hg_r[:, v], hg_ss[:, v], 1.0 / HG_D, EPS, ALU.mult, ALU.add).then_inc(sem("pool_rs"), 1)
                pool.wait_ge(sem("pool_rs"), 3 + rnd)
                pool.tensor_tensor(hg_r[:, v], hg_r[:, v], mhalf[:, 0:24], ALU.pow).then_inc(sem("hg_r"), 1)

            pool.wait_ge(sem("aug_ones"), 2)
            pool.wait_ge(step("cum_ready"), nth("cum_ready"))
            for h in range(FOX_H):
                pool.dma_start(qaug[64:65, h], cum[h:h + 1]).then_inc(sem("aug_in"), 16)
                pool.dma_start(kaug[65:66, h], ncum[h:h + 1]).then_inc(sem("aug_in"), 16)
            pool.wait_ge(sem("w_out_in"), 16)
            pool.wait_ge(sem("late_in"), 16)
            for k in range(KD):
                last = pool.tensor_scalar(w_out[:, k], w_out[:, k], wrow[:, k:k + 1], None, ALU.mult)
            last.then_inc(step("w_scaled"), 1)
            pool.wait_ge(sem("aug_in"), 16 * 2 * FOX_H)
            for v, src in ((gmb, mod_d[2:3]), (b2b, mod_d[3:4]), (a2b, mod_d[4:5]), (nfw, A["norms"][1:2])):
                pool.dma_start(v, src.to_broadcast([P, D])).then_inc(sem("mod2_in"), 16)
            pool.wait_ge(sem("mod2_in"), 64)
            pool.tensor_tensor(a2b, a2b, nfw, ALU.mult).then_inc(step("a2_mul"), 1)
            pool.wait_ge(step("a2_mul"), nth("a2_mul"))
            pool.tensor_tensor(a2b, a2b, nfw, ALU.add).then_inc(step("a2_ready"), 1)
            for i in range(NT):
                pool.wait_ge(sem("fssq"), i + 1)
                pool.tensor_scalar(frstd[:, i:i + 1], fssq[:, i:i + 1], 1.0 / FOX_W, EPS, ALU.mult, ALU.add).then_inc(sem("pool_rs"), 1)
                pool.wait_ge(sem("pool_rs"), 5 + i)
                pool.tensor_tensor(frstd[:, i:i + 1], frstd[:, i:i + 1], mhalf[:, 0:1], ALU.pow).then_inc(sem("frstd"), 1)

            def power(ss, r, n):
                n_pow[0] += 1
                pool.tensor_scalar(r, ss, 1.0 / n, EPS, ALU.mult, ALU.add).then_inc(sem("pool_rs"), 1)
                pool.wait_ge(sem("pool_rs"), n_pow[0])
                return pool.tensor_tensor(r, r, mhalf[:, 0:1], ALU.pow)

            n_pow = [4 + NT]
            for i in range(NT):
                pool.wait_ge(sem("ssq2"), i + 1)
                power(ssq2[:, i:i + 1], rstd2[:, i:i + 1], D).then_inc(sem("rstd2"), 1)
                pool.wait_ge(sem("h2_mul"), i + 1)
                pool.tensor_tensor(h2[i % 2], h2[i % 2], b2b, ALU.add).then_inc(sem("h2_ready"), 1)
            pool.dma_start(gfb, mod_d[5:6].to_broadcast([P, D])).then_inc(sem("last_in"), 16)
            pool.dma_start(fnw, A["norms"][2:3].to_broadcast([P, D])).then_inc(sem("last_in"), 16)
            pool.wait_ge(step("list_zero"), nth("list_zero"))
            pool.dma_start(list_d.rearrange("(a b) o -> a (b o)", a=P), tok_l).then_inc(sem("list_set"), 16)
            pool.tensor_copy(tok_i, cst[:, C_TOK:C_TOK + NT]).then_inc(step("tok_ready"), 1)
            pool.wait_ge(step("tok_ready"), nth("tok_ready"))
            pool.wait_ge(sem("list_set"), 16)
            pool.wait_ge(sem("slot_ready"), 2)
            for i in range(NT):
                for v in (slot_a, slot_b):
                    pool.indirect_dma_start(out=list_d, out_offset=bass.IndirectOffsetOnAxis(ap=v[:, i:i + 1], axis=0),
                                            in_=tok_i[:, i:i + 1], in_offset=None).then_inc(sem("list_out"), 16)
            pool.wait_ge(sem("list_out"), 16 * 2 * NT)
            pool.dma_start(tok_l, list_d.rearrange("(t p) o -> p (t o)", p=P), allow_slow_non_contiguous=True).then_inc(sem("tok_in"), 16)
            pool.wait_ge(sem("tok_in"), 16)
            pool.wait_ge(sem("h2_out0"), 16 * NT // 2)
            pool.wait_ge(sem("h2_out1"), 16 * NT // 2)
            pool.wait_ge(sem("mix_mm"), NT)
            for t in range(TILES):
                if t >= 4:
                    pool.wait_ge(sem("moe_T"), t - 3)
                pool.indirect_dma_start(out=rows[t % 4], out_offset=None, in_=h2_d,
                                        in_offset=bass.IndirectOffsetOnAxis(ap=tok_l[:, t:t + 1], axis=0)).then_inc(sem(f"row_in{t % 4}"), 16)
            pool.wait_ge(sem("moe_gu"), TILES)
            pool.wait_ge(sem("moe_dn"), TILES)
            for i in range(2):
                pool.wait_ge(sem(f"y_out{i}"), 16 * ((TILES + 1 - i) // 2))

            def fetch(i):
                b = i % NY
                if i >= NY:
                    pool.wait_ge(sem("x3_ready"), i - NY + 1)
                for w, v, n in ((y_a, slot_a, "a"), (y_b, slot_b, "b")):
                    pool.indirect_dma_start(out=w[b], out_offset=None, in_=y_d,
                                            in_offset=bass.IndirectOffsetOnAxis(ap=v[:, i:i + 1], axis=0)).then_inc(sem(f"y{n}_in{b}"), 16)

            for i in range(NY):
                fetch(i)
            for i in range(NT):
                pool.wait_ge(sem("ssq3"), i + 1)
                power(ssq3[:, i:i + 1], rstd3[:, i:i + 1], D).then_inc(sem("rstd3"), 1)
                if i + NY < NT:
                    fetch(i + NY)

        @block.scalar
        def _(act):
            act.wait_ge(sem("c_in"), 16)
            act.activation(cact, cact, ACT.Silu).then_inc(step("cact"), 1)
            act.wait_ge(sem("s5_in"), 16)
            act.activation(dt, dt, ACT.Exp).then_inc(step("s5_dt"), 1)
            act.wait_ge(step("s5_ph"), nth("s5_ph"))
            act.activation(p_mag, p_mag, ACT.Exp).then_inc(sem("s5_pw"), 1)
            for w in (p_re, p_im):
                act.activation(w, w, ACT.Sin, scale=TWO_PI).then_inc(sem("s5_pw"), 1)
            act.wait_ge(step("s5_rot"), nth("s5_rot"))
            for w in (s5_cos, s5_sin):
                act.activation(w, w, ACT.Sin, scale=TWO_PI).then_inc(sem("s5_cs"), 1)
            act.wait_ge(sem("x_in"), 16)
            for i in range(NT):
                act.activation(a1b, x_sb[:, i], ACT.Square, accum_out=ssq[:, i:i + 1]).then_inc(sem("ssq_x"), 1)
                act.wait_ge(sem("ssq_x"), i + 1)
            act.wait_ge(sem("kern_out"), 16)
            for i in range(NT):
                act.wait_ge(sem("h_tr"), i + 1)
                act.copy(hT[:, 0:4, i * P:(i + 1) * P],
                         bank(4 + 2 * (i % 2)).rearrange("p (k t) -> p k t", t=P)).then_inc(sem("hT_act"), 1)

            def take(name, out_of):
                for u in unit_range(name):
                    g, where = UNITS[u]
                    act.wait_ge(sem("win_mm"), u + 1)
                    for o, i, f, sc in out_of(where, bank(u % WIN_BANKS)):
                        last = act.activation(o, i, f, scale=sc)
                    last.then_inc(sem("ev_act"), 1)

            take("hq", lambda w, b: [(hq[:, w[0], 512 * w[1]:512 * w[1] + 512], b, ACT.Silu, 1.0)])
            act.wait_ge(sem("mod_out"), 32)
            take("hg", lambda i, b: [(hgate[:, i], b[:, 0:HG_W], ACT.Silu, 1.0)])
            act.wait_ge(step("s5_y_mm"), nth("s5_y_mm"))
            for b in range(4):
                m0 = 4 * (b % 2)
                act.activation(s5_y.rearrange("p s (m g c) -> p g m s c", g=2, c=S5_C)[:, b // 2, m0:m0 + 4],
                               bank(4 + b).rearrange("p (m s c) -> p m s c", m=4, s=S5_L), ACT.Gelu_apprx_tanh).then_inc(sem("s5_gelu"), 1)
            act.wait_ge(step("s5_glu_mm"), nth("s5_glu_mm"))
            act.activation(s5_gate.rearrange("p s n -> p (s n)"), bank(4, 4), ACT.Sigmoid).then_inc(step("s5_gate"), 1)
            take("fq", lambda w, b: [(qaug[0:64, 2 * w[0] + par, 512 * w[1]:512 * w[1] + 512], b[64 * par:64 * par + 64], ACT.Copy, FOX_D ** -0.5)
                                     for par in range(2)])
            act.wait_ge(sem("ev_dve"), evacuated("dve", unit_range("hf")[-1]))
            act.wait_ge(step("s5_o_tr"), nth("s5_o_tr"))
            act.activation(hk, hb, ACT.Sigmoid, scale=-1.0).then_inc(step("hk_ready"), 1)
            act.wait_ge(step("hk_ready"), nth("hk_ready"))
            for m in range(HG_M):
                if m:
                    act.wait_ge(sem("hg_lf"), m)
                for c, (f, src, sc, bias) in enumerate(((ACT.Abs, hb[:, m], 1.0, 0.0), (ACT.Exp, hg_tmp, -1.0, 0.0), (ACT.Ln, hg_tmp, 1.0, 1.0))):
                    last = act.activation(hg_tmp, src, f, scale=sc, bias=bias)
                    last.then_inc(sem("hg_ln" if c == 2 else "hg_abs"), 1)
                    if c < 2:
                        act.wait_ge(sem("hg_abs"), 2 * m + c + 1)

            act.wait_ge(sem("flog"), 1)
            for c, (f, src, sc, bias) in enumerate(((ACT.Abs, flog, 1.0, 0.0), (ACT.Exp, fln, -1.0, 0.0), (ACT.Ln, fln, 1.0, 1.0))):
                act.activation(fln, src, f, scale=sc, bias=bias).then_inc(sem("fln"), 1)
                act.wait_ge(sem("fln"), c + 1)
            act.wait_ge(sem("hb_ready"), HG_M * NT)
            act.wait_ge(sem("win_mm"), len(UNITS))
            act.activation(qe, hb, ACT.Exp).then_inc(step("e_b"), 1)
            act.activation(efin.rearrange("p (m n) -> p m n", m=HG_M), hb[:, :, P - 1::P], ACT.Exp).then_inc(step("efin"), 1)
            act.wait_ge(step("d_kb"), nth("d_kb"))
            act.activation(ke, ke, ACT.Exp).then_inc(step("e_kb"), 1)
            for c in range(2 * n_lev):
                act.wait_ge(sem("lev_d"), c + 1)
                act.activation(lev[c % 2], lev[c % 2], ACT.Exp).then_inc(sem("lev_exp"), 1)

            def fox_take(i):
                act.wait_ge(sem("fo_tr"), i + 1)
                act.copy(cFox[:, :, i * P:(i + 1) * P], bank(6 + i % 2)[:, 0:FOX_W].rearrange("p (m t) -> p m t", m=3)).then_inc(sem("cFox_ready"), 1)

            act.wait_ge(sem("cHg_ready"), NT)
            for u, (i, h) in enumerate(units):
                act.wait_ge(sem("f_max"), u + 1)
                if u >= 2:
                    act.wait_ge(sem("f_T"), u - 1)
                w = (i + 1) * P
                act.activation(prob[u % 2][:, 0:w], psum[:, 1024 * (u % 2):1024 * (u % 2) + w], ACT.Exp, bias=negmax[:, u:u + 1],
                               accum_out=rowsum[:, u:u + 1]).then_inc(sem("f_exp"), 1)
                if i >= 4:
                    act.wait_ge(sem("f_T"), u + 1)
                    if u >= 2:
                        act.wait_ge(sem("f_pv"), u - 1)
                    act.copy(probT[u % 2][:, 4:i + 1], bank(5)[:, 0:(i - 3) * P].rearrange("p (k q) -> p k q", q=P)).then_inc(sem("fT_act"), 1)
                if i >= 1 and h == 5:
                    fox_take(i - 1)
            fox_take(NT - 1)

            act.wait_ge(sem("f_pv"), len(units))
            for i in range(NT):
                if i >= 1:
                    act.wait_ge(sem("ssq2"), i)
                act.wait_ge(sem("x2_ready"), i + 1)
                act.activation(sq2, x2[:, i], ACT.Square, accum_out=ssq2[:, i:i + 1]).then_inc(sem("ssq2"), 1)
                act.wait_ge(sem("h2_tr"), i + 1)
                if i >= 2:
                    act.wait_ge(sem("route_mm"), i - 1)
                act.copy(h2T[i % 2][:, 0:4], bank(4).rearrange("p (k t) -> p k t", t=P)).then_inc(sem("h2T_act"), 1)
            act.wait_ge(step("rt_sub"), nth("rt_sub"))
            act.activation(rt[1], rt[0], ACT.Exp).then_inc(step("rt_exp"), 1)

            def take_rows(t, j):
                act.wait_ge(sem("moe_T"), t + 1)
                if not (isinstance(t, int) and t < 2):
                    act.wait_ge(sem("moe_gu"), t - 1)
                act.copy(rowT[j % 2][:, 0:4], bank(2).rearrange("p (k t) -> p k t", t=P)).then_inc(sem("rowT_act"), 1)

            def take_answer(t, j, r):
                act.wait_ge(sem("moe_dn"), t + 1)
                if not (isinstance(t, int) and t < 2):
                    act.wait_ge(sem(f"y_out{j % 2}"), 32 * r + 16 * (j // 2))
                act.copy(answer[j % 2][:, 0:512], bank(5)).then_inc(sem("y_act"), 1)
                act.wait_ge(sem("y_act"), t + 1)
                act.wait_ge(sem("y_dve"), t + 1)
                act.dma_start(y_d[bass.ds(t * P, P)], answer[j % 2]).then_inc(sem(f"y_out{j % 2}"), 16)

            def gate(t, j, r):
                act.wait_ge(sem("moe_gu"), t + 1)
                if not (isinstance(t, int) and t < 2):
                    act.wait_ge(sem("hid_ready"), t - 1)
                act.activation(silu[j % 2], bank(j % 2)[:, 0:FF], ACT.Silu).then_inc(sem("silu_ready"), 1)
                if not (isinstance(t, int) and t == TILES - 1):
                    take_rows(t + 1, (j + 1) % 4)
                if not (isinstance(t, int) and t == 0):
                    take_answer(t - 1, (j - 1) % 4, r if j else r - 1)

            take_rows(0, 0)
            each_tile(act, gate)
            take_answer(TILES - 1, (TILES - 1) % 4, TILES // 4)

            for i in range(NT + 1):
                if i < NT:
                    b = i % NY
                    act.wait_ge(sem(f"ya_in{b}"), 16 * (i // NY + 1))
                    act.activation(y_a[b], y_a[b], ACT.Copy, scale=wgt_a[:, i:i + 1]).then_inc(sem("ya_scaled"), 1)
                if i >= 1:
                    act.wait_ge(sem("x3_ready"), i)
                    if i >= 2:
                        act.wait_ge(sem("ssq3"), i - 1)
                    act.activation(sq3, x2[:, i - 1], ACT.Square, accum_out=ssq3[:, i - 1:i]).then_inc(sem("ssq3"), 1)

        @block.vector
        def _(dve):
            n_own = [0]

            def link(ins):
                n_own[0] += 1
                ins.then_inc(sem("dve_own"), 1)
                dve.wait_ge(sem("dve_own"), n_own[0])

            def mod_rows(a, b):
                for n in range(a, b):
                    row = mod_row[:, n * ADA_N:(n + 1) * ADA_N]
                    dve.wait_ge(sem("ada_mm"), n + 1)
                    dve.tensor_tensor(row, bank(n % 4)[0:1], row, ALU.add).then_inc(sem("mod_row"), 1)

            dve.wait_ge(sem("const_in"), 32)
            dve.wait_ge(step("s5_dt"), nth("s5_dt"))
            link(dve.tensor_tensor(lr, are, dt, ALU.mult))
            link(dve.tensor_tensor(th, aim, dt, ALU.mult))
            link(dve.tensor_scalar(th, th, 1.0 / (2 * np.pi), None, ALU.mult))

            def whole_turns_off(x, scratch):
                link(dve.tensor_scalar(scratch, x, ROUND, ROUND, ALU.add, ALU.subtract))
                return dve.tensor_tensor(x, x, scratch, ALU.subtract)

            link(whole_turns_off(th, u0))
            n17 = cst[:, C_POW:C_POW + 17].unsqueeze(1).to_broadcast([P, S5_M, 17])
            link(dve.tensor_tensor(p_mag, b3(lr, 17), n17, ALU.mult))
            link(dve.tensor_tensor(p_im, b3(th, 17), n17, ALU.mult))
            link(dve.tensor_scalar(p_re, p_im, 0.25, None, ALU.add))
            link(whole_turns_off(p_im, p_tmp))
            whole_turns_off(p_re, p_tmp).then_inc(step("s5_ph"), 1)
            link(dve.tensor_scalar(ph8, th, float(S5_L), None, ALU.mult))
            link(whole_turns_off(ph8, u0))
            jrow = cst[:, C_J:C_J + P].unsqueeze(1).to_broadcast([P, S5_M, S5_J])
            link(dve.tensor_tensor(s5_sin.rearrange("p (m j) -> p m j", m=S5_M), b3(ph8, S5_J), jrow, ALU.mult))
            link(dve.tensor_scalar(s5_cos, s5_sin, 0.25, None, ALU.add))
            link(whole_turns_off(s5_sin, s5_tab[0]))
            whole_turns_off(s5_cos, s5_tab[0]).then_inc(step("s5_rot"), 1)
            dve.wait_ge(sem("s5_pw"), 3)
            link(dve.tensor_tensor(p_re, p_re, p_mag, ALU.mult))
            link(dve.tensor_tensor(p_im, p_im, p_mag, ALU.mult))
            link(dve.tensor_scalar(am1, p_re[:, :, 1], -1.0, None, ALU.add))
            link(dve.tensor_tensor(u0, are, are, ALU.mult))
            link(dve.tensor_tensor(u1, aim, aim, ALU.mult))
            link(dve.tensor_tensor(den, u0, u1, ALU.add))
            link(dve.reciprocal(den, den))
            link(dve.tensor_tensor(u0, am1, are, ALU.mult))
            link(dve.tensor_tensor(u1, p_im[:, :, 1], aim, ALU.mult))
            link(dve.tensor_tensor(u0, u0, u1, ALU.add))
            link(dve.tensor_tensor(wr, u0, den, ALU.mult))
            link(dve.tensor_tensor(u0, p_im[:, :, 1], are, ALU.mult))
            link(dve.tensor_tensor(u1, am1, aim, ALU.mult))
            link(dve.tensor_tensor(u0, u0, u1, ALU.subtract))
            link(dve.tensor_tensor(wi, u0, den, ALU.mult))

            def complex_mul(out_re, out_im, ar, ai, br, bi, shape, minus_im=False):
                n = int(np.prod(shape))
                names = "xyz"[:len(shape)]
                t, v = [w[:, 0:n].rearrange(f"p ({' '.join(names)}) -> p {' '.join(names)}",
                                            **{k: q for k, q in zip(names[1:], shape[1:])}) for w in s5_tab]
                dve.tensor_tensor(t, ar, br, ALU.mult)
                link(dve.tensor_tensor(v, ai, bi, ALU.mult))
                link(dve.tensor_tensor(out_re, t, v, ALU.subtract))
                dve.tensor_tensor(t, ar, bi, ALU.mult)
                link(dve.tensor_tensor(v, ai, br, ALU.mult))
                if minus_im:
                    return dve.scalar_tensor_tensor(out=out_im, in0=t, scalar=-1.0, in1=v, op0=ALU.mult, op1=ALU.subtract)
                return dve.tensor_tensor(out_im, t, v, ALU.add)

            link(complex_mul(s5_bb[:, 0], s5_bb[:, 1], b3(wr, S5_C), b3(wi, S5_C), s5_B[:, 0], s5_B[:, 1], (S5_M, S5_C)))
            full = [P, S5_M, S5_L, S5_C]
            complex_mul(s5_BA[:, 0], s5_BA[:, 1],
                        p_re[:, :, 9:17].unsqueeze(3).to_broadcast(full), p_im[:, :, 9:17].unsqueeze(3).to_broadcast(full),
                        s5_bb[:, 0].unsqueeze(2).to_broadcast(full), s5_bb[:, 1].unsqueeze(2).to_broadcast(full),
                        full[1:]).then_inc(step("s5_BA"), 1)
            dve.wait_ge(step("s5_BA"), nth("s5_BA"))
            for mh in range(2):
                ms = slice(4 * mh, 4 * mh + 4)
                nine = [P, 4, 9, S5_C]
                last = complex_mul(s5_CA[:, 0, ms], s5_CA[:, 1, ms],
                                   p_re[:, ms, 0:9].unsqueeze(3).to_broadcast(nine), p_im[:, ms, 0:9].unsqueeze(3).to_broadcast(nine),
                                   s5_Ct[:, 0, ms].unsqueeze(2).to_broadcast(nine), s5_Ct[:, 1, ms].unsqueeze(2).to_broadcast(nine),
                                   nine[1:], minus_im=True)
                link(last)
            dve.tensor_copy(s5_R.rearrange("p (m j) -> p m j", m=S5_M), b3(p_mag[:, :, 8], S5_J)).then_inc(step("s5_CA"), 1)
            dve.wait_ge(step("s5_CA"), nth("s5_CA"))
            link(dve.memset(s5_R.rearrange("p (m j) -> p m j", m=S5_M)[:, :, 0:1], 0.0))

            dve.wait_ge(sem("ada_b_in"), 16)
            mod_rows(0, 4)
            dve.wait_ge(sem("mod1_in"), 32)
            dve.wait_ge(sem("nmw_in"), 16)
            link(dve.scalar_tensor_tensor(out=a1b, in0=a1b, scalar=1.0, in1=nmw, op0=ALU.add, op1=ALU.mult))
            dve.wait_ge(step("rstd_x"), nth("rstd_x"))
            for i in range(NT):
                dve.scalar_tensor_tensor(out=x_sb[:, i], in0=x_sb[:, i], scalar=rstd[:, i:i + 1], in1=a1b,
                                         op0=ALU.mult, op1=ALU.mult).then_inc(sem("h_mul"), 1)
            dve.wait_ge(step("s5_W_tr"), nth("s5_W_tr"))
            for b in range(4):
                dve.tensor_copy(s5_W.rearrange("p m a x -> p (m a x)")[:, 512 * b:512 * b + 512], bank(4 + b)).then_inc(sem("s5_W"), 1)
            mod_rows(4, 6)
            dve.wait_ge(step("s5_kern"), nth("s5_kern"))
            dve.wait_ge(step("kz_zero"), nth("kz_zero"))
            for par in range(2):
                link(dve.tensor_copy(kz.rearrange("c (m g) x -> c g m x", g=2)[:, par, :, P:2 * P],
                                     bank(4 + 2 * par, 2)[0:S5_C].rearrange("c (m x) -> c m x", m=S5_M)))
            dd = s5_tab[0][0:S5_C, 0:S5_G * S5_C].rearrange("c (g x) -> c g x", g=S5_G)
            link(dve.tensor_tensor(dd, b3(s5_D, S5_C), cst[0:S5_C, 0:S5_C].unsqueeze(1).to_broadcast([S5_C, S5_G, S5_C]), ALU.mult))
            dve.tensor_tensor(kz[:, :, P:P + S5_C], kz[:, :, P:P + S5_C], dd, ALU.add).then_inc(step("kz_full"), 1)
            mod_rows(6, 12)
            dve.wait_ge(sem("kern_out"), 16)
            for i in range(NT):
                dve.wait_ge(sem("h_tr"), i + 1)
                dve.tensor_copy(hT[:, 4:8, i * P:(i + 1) * P],
                                bank(5 + 2 * (i % 2)).rearrange("p (k t) -> p k t", t=P)).then_inc(sem("hT_dve"), 1)

            def take(name, out_of):
                for u in unit_range(name):
                    g, where = UNITS[u]
                    dve.wait_ge(sem("win_mm"), u + 1)
                    for o, i in out_of(where, bank(u % WIN_BANKS)):
                        last = dve.tensor_copy(o, i)
                    last.then_inc(sem("ev_dve"), 1)

            take("su", lambda st, b: [(s5_Z[:, :, st], b[:, 0:S5_W].rearrange("p (g c) -> p g c", g=S5_G))])
            dve.wait_ge(step("s5_U_tr"), nth("s5_U_tr"))
            for b in range(4):
                dve.tensor_copy(s5_U.rearrange("p g j -> p (g j)")[:, 512 * b:512 * b + 512], bank(4 + b)).then_inc(sem("s5_U"), 1)
            dve.wait_ge(sem("mod_out"), 32)
            take("hi", lambda i, b: [(hv[:, i], b[:, 0:HG_W])])
            dve.wait_ge(step("s5_V_mm"), nth("s5_V_mm"))
            dve.wait_ge(sem("s5_cs"), 2)
            v_re, v_im = bank(4, 2), bank(6, 2)
            t, v = s5_t
            dve.tensor_tensor(t, v_re, s5_cos, ALU.mult)
            link(dve.tensor_tensor(v, v_im, s5_sin, ALU.mult))
            link(dve.tensor_tensor(s5_V[:, 0], t, v, ALU.add))
            dve.tensor_tensor(t, v_im, s5_cos, ALU.mult)
            link(dve.tensor_tensor(v, v_re, s5_sin, ALU.mult))
            link(dve.tensor_tensor(s5_V[:, 1], t, v, ALU.subtract))
            for a in range(2):
                link(dve.tensor_tensor_scan(out=s5_V[:, a], data0=s5_R, data1=s5_V[:, a], initial=0.0, op0=ALU.mult, op1=ALU.add))
            xr, xi = s5_V[:, 0], s5_V[:, 1]
            mj = lambda w: w.rearrange("p (m j) -> p m j", m=S5_M)
            for a, (op, x0, x1) in enumerate(((ALU.subtract, xr, xi), (ALU.add, xi, xr))):
                dve.tensor_tensor(t, x0, s5_cos, ALU.mult)
                link(dve.tensor_tensor(v, x1, s5_sin, ALU.mult))
                dve.memset(s5_X[a][:, :, 0:1], 0.0).then_inc(sem("s5_X0"), 1)
                dve.wait_ge(sem("s5_X0"), a + 1)
                dve.tensor_tensor(s5_X[a][:, :, 1:S5_J], mj(t)[:, :, 0:S5_J - 1], mj(v)[:, :, 0:S5_J - 1], op).then_inc(sem("s5_X"), 1)
                dve.wait_ge(sem("s5_X"), a + 1)
            take("hf", lambda w, b: [(hb[:, w[0], 512 * w[1]:512 * w[1] + 512], b)])
            dve.wait_ge(step("s5_y_tr"), nth("s5_y_tr"))
            for b in range(4):
                dve.tensor_copy(s5_yT.rearrange("p c s j -> p (c s j)")[:, 512 * b:512 * b + 512], bank(4 + b)).then_inc(sem("s5_yT"), 1)
            take("fv", lambda i, b: [(fv[:, i], b[:, 0:VW])])
            dve.wait_ge(sem("late_in"), 16)
            dve.wait_ge(sem("ev_dve"), evacuated("dve", unit_range("fv")[-1]))
            f3 = flog.rearrange("p (i h) -> p i h", h=FOX_H)
            dve.tensor_tensor(f3, fv[:, :, FOX_W:VW], fbias.unsqueeze(1).to_broadcast([P, NT, FOX_H]), ALU.add).then_inc(sem("flog"), 1)
            dve.wait_ge(step("s5_gate"), nth("s5_gate"))
            link(dve.tensor_tensor(s5_y, s5_y, s5_gate, ALU.mult))
            link(dve.tensor_tensor(s5_sq, s5_y, s5_y, ALU.mult))
            dve.tensor_reduce(sssq, s5_sq, AX_X, ALU.add).then_inc(step("sssq"), 1)
            dve.wait_ge(step("srstd"), nth("srstd"))
            dve.tensor_tensor(s5_y, s5_y, b3(srstd, S5_W), ALU.mult).then_inc(step("s5_o"), 1)
            dve.wait_ge(step("s5_o_tr"), nth("s5_o_tr"))
            for b in range(4):
                c, s0 = b // 2, 4 * (b % 2)
                dve.tensor_copy(cS5[:, c].rearrange("p (j s) -> p s j", s=S5_L)[:, s0:s0 + 4],
                                bank(4 + b).rearrange("p (s j) -> p s j", s=4)).then_inc(sem("s5_done"), 1)
            for m in range(HG_M):
                dve.wait_ge(sem("hg_ln"), m + 1)
                dve.scalar_tensor_tensor(out=hb[:, m], in0=hb[:, m], scalar=0.0, in1=hg_tmp, op0=ALU.min, op1=ALU.subtract).then_inc(sem("hg_lf"), 1)
                dve.wait_ge(sem("hg_lf"), m + 1)
                for n in range(NT):
                    dve.tensor_tensor_scan(out=hb[:, m, n * P:(n + 1) * P], data0=ones, data1=hb[:, m, n * P:(n + 1) * P], initial=0.0,
                                           op0=ALU.mult, op1=ALU.add).then_inc(sem("hb_ready"), 1)
            take("fk", lambda w, b: [(kaug[0:64, 2 * w[0] + par, 512 * w[1]:512 * w[1] + 512], b[64 * par:64 * par + 64]) for par in range(2)])

            def take_scores(rnd, l):
                for h in range(HG_H):
                    c = (rnd * (1 + n_lev) + l) * HG_H + h
                    if l:
                        dve.wait_ge(sem("hg_taken"), c - HG_H + 1)
                    dve.wait_ge(sem("hg_mm"), c + 1)
                    b = bank(c % 4).rearrange("p (n t) -> p n t", n=4)
                    if l == 0:
                        dve.tensor_tensor(sT[:, h], b, ident.unsqueeze(1).to_broadcast([P, 4, P]), ALU.mult).then_inc(sem("hg_taken"), 1)
                    else:
                        dve.copy_predicated(sT[:, h], masks[:, l].unsqueeze(1).to_broadcast([P, 4, P]), b).then_inc(sem("hg_taken"), 1)

            def halves(v, l):
                return v.rearrange("p m (b two x) -> p m b two x", two=2, x=LEVELS[l - 1])

            dve.wait_ge(sem("fln"), 3)
            dve.scalar_tensor_tensor(out=flog, in0=flog, scalar=0.0, in1=fln, op0=ALU.min, op1=ALU.subtract).then_inc(sem("flog"), 1)
            dve.tensor_copy(ident16[:], ident).then_inc(sem("mask16"), 1)
            dve.tensor_copy(neg16[:], cst[:, C_NEG:C_NEG + P]).then_inc(sem("mask16"), 1)
            dve.wait_ge(step("e_b"), nth("e_b"))
            dve.tensor_tensor(qe, qe, hq, ALU.mult).then_inc(step("qe_ready"), 1)
            dve.wait_ge(step("e_kb"), nth("e_kb"))
            dve.tensor_tensor(ke, ke, hk, ALU.mult).then_inc(step("ke_ready"), 1)
            for rnd in range(2):
                rs = slice(512 * rnd, 512 * rnd + 512)
                if rnd:
                    dve.wait_ge(sem("hg_o_mm"), rnd)
                take_scores(rnd, 0)
                for n in range(4):
                    dve.wait_ge(sem("ke_tr"), 4 * rnd + n + 1)
                    dve.tensor_copy(keT[4 * rnd + n], bank(4 + n)[:, 0:HG_W]).then_inc(sem("keT_ready"), 1)
                for n in range(4):
                    c = 4 * rnd + n
                    if c == NT - 1:
                        break
                    dve.wait_ge(sem("dS_mm"), min(4 * rnd + 2 * (n // 2) + 2, NT - 1))
                    dS = psum[:, 2048 + 512 * (n // 2) + 192 * (n % 2):2048 + 512 * (n // 2) + 192 * (n % 2) + 192]
                    if c == 0:
                        dve.tensor_copy(hg_S[:, 0], dS).then_inc(sem("hg_S"), 1)
                    else:
                        dve.wait_ge(sem("hg_S"), c)
                        link(dve.tensor_tensor(hg_S[:, c].rearrange("p (m v) -> p m v", m=HG_M), hg_S[:, c - 1].rearrange("p (m v) -> p m v", m=HG_M),
                                               b3(efin.rearrange("p (m n) -> p m n", m=HG_M)[:, :, c], HG_D), ALU.mult))
                        dve.tensor_tensor(hg_S[:, c], hg_S[:, c], dS, ALU.add).then_inc(sem("hg_S"), 1)
                for l in range(1, 1 + n_lev):
                    x = lev[(rnd * n_lev + l - 1) % 2]
                    dve.wait_ge(sem("lev_exp"), rnd * n_lev + l)
                    r = halves(x, l)[:, :, :, 1]
                    dve.tensor_tensor(r, r, halves(hq[:, :, rs], l)[:, :, :, 1], ALU.mult).then_inc(sem("lev_q"), 1)
                    if l > 1:
                        take_scores(rnd, l - 1)
                take_scores(rnd, n_lev)
                dve.wait_ge(sem("hg_o_mm"), rnd + 1)
                for b in range(4):
                    par, n0 = b // 2, 2 * (b % 2)
                    dve.tensor_copy(hg_o.rearrange("p (n m g) v -> p n m g v", m=HG_M, g=2)[:, n0:n0 + 2, :, par],
                                    bank(4 + b)[:, 0:384].rearrange("p (n m v) -> p n m v", n=2, m=HG_M)).then_inc(sem("hg_o_taken"), 1)
                dve.wait_ge(sem("hg_o_taken"), 4 * rnd + 4)
                link(dve.tensor_tensor(hg_sq, hg_o, hg_o, ALU.mult))
                dve.tensor_reduce(hg_ss[:, 24 * rnd:24 * rnd + 24], hg_sq, AX_X, ALU.add).then_inc(sem("hg_ss"), 1)
                dve.wait_ge(sem("hg_r"), rnd + 1)
                link(dve.tensor_tensor(hg_o, hg_o, b3(hg_r[:, 24 * rnd:24 * rnd + 24], HG_D), ALU.mult))
                g = hgate[:, 4 * rnd:4 * rnd + 4].rearrange("p n w -> p (n w)")
                dve.tensor_tensor(g, hg_o.rearrange("p a v -> p (a v)"), g, ALU.mult).then_inc(sem("hg_gated"), 1)
            for n in range(NT):
                dve.wait_ge(sem("hg_o_tr"), n + 1)
                dve.tensor_copy(cHg[:, :, n * P:(n + 1) * P], bank(4 + n % 4)[:, 0:HG_W].rearrange("p (m t) -> p m t", m=HG_M)).then_inc(sem("cHg_ready"), 1)

            dve.wait_ge(step("f_tr"), nth("f_tr"))
            link(dve.tensor_tensor_scan(out=cum, data0=cst[0:FOX_H, C_ONE:C_ONE + 1].to_broadcast([FOX_H, T]), data1=bank(4, 2)[0:FOX_H],
                                        initial=0.0, op0=ALU.mult, op1=ALU.add))
            dve.tensor_scalar(ncum, cum, -1.0, None, ALU.mult).then_inc(step("cum_ready"), 1)

            def maxima(u):
                i, h = units[u]
                dve.wait_ge(sem("f_qk"), u + 1)
                dve.tensor_reduce(negmax[:, u:u + 1], psum[:, 1024 * (u % 2):1024 * (u % 2) + (i + 1) * P], AX_X, ALU.max, negate=True).then_inc(sem("f_max"), 1)

            def fox_norm(i):
                dve.wait_ge(sem("f_pv"), FOX_H * (i + 1))
                dve.wait_ge(sem("f_exp"), FOX_H * (i + 1))
                hs = slice(FOX_H * i, FOX_H * (i + 1))
                link(dve.reciprocal(rinv[:, hs], rowsum[:, hs]))
                o = fo[i % 2]
                if i >= 2:
                    dve.wait_ge(sem("fo_tr"), i - 1)
                link(dve.tensor_tensor(o.rearrange("p (h d) -> p h d", h=FOX_H), bank(6 + i % 2)[:, 0:FOX_W].rearrange("p (h d) -> p h d", h=FOX_H),
                                       b3(rinv[:, hs], FOX_D), ALU.mult))
                link(dve.tensor_tensor(fsq, o, o, ALU.mult))
                dve.tensor_reduce(fssq[:, i:i + 1], fsq, AX_X, ALU.add).then_inc(sem("fssq"), 1)

            def fox_scale(i):
                dve.wait_ge(sem("frstd"), i + 1)
                dve.tensor_scalar(fo[i % 2], fo[i % 2], frstd[:, i:i + 1], None, ALU.mult).then_inc(sem("fo_ready"), 1)

            maxima(0)
            for u in range(len(units)):
                i, h = units[u]
                if u + 1 < len(units):
                    maxima(u + 1)
                dve.wait_ge(sem("f_T"), u + 1)
                if u >= 2:
                    dve.wait_ge(sem("f_pv"), u - 1)
                w = min(4, i + 1)
                dve.tensor_copy(probT[u % 2][:, 0:w], bank(4)[:, 0:w * P].rearrange("p (k q) -> p k q", q=P)).then_inc(sem("fT_dve"), 1)
                if i >= 1 and h == 1:
                    fox_norm(i - 1)
                if i >= 1 and h == 2:
                    fox_scale(i - 1)
            fox_norm(NT - 1)
            fox_scale(NT - 1)

            dve.wait_ge(sem("x2_in"), 16)
            dve.wait_ge(sem("mod2_in"), 64)
            dve.wait_ge(sem("f_pv"), len(units))

            def add_mix(i):
                dve.wait_ge(sem("mix_mm"), i + 1)
                if i >= 2:
                    dve.wait_ge(sem("x2_ready"), i - 1)
                dve.tensor_tensor(mix_t[i % 2], bank(2 * (i % 2), 2), gmb, ALU.mult).then_inc(sem("mix_taken"), 1)
                dve.wait_ge(sem("mix_taken"), i + 1)
                dve.tensor_tensor(x2[:, i], x2[:, i], mix_t[i % 2], ALU.add).then_inc(sem("x2_ready"), 1)

            add_mix(0)
            for i in range(NT):
                dve.wait_ge(sem("rstd2"), i + 1)
                dve.wait_ge(step("a2_ready"), nth("a2_ready"))
                if i >= 2:
                    dve.wait_ge(sem(f"h2_out{i % 2}"), 16 * (i // 2))
                    dve.wait_ge(sem("h2_tr"), i - 1)
                dve.scalar_tensor_tensor(out=h2[i % 2], in0=x2[:, i], scalar=rstd2[:, i:i + 1], in1=a2b, op0=ALU.mult, op1=ALU.mult).then_inc(sem("h2_mul"), 1)
                if i + 1 < NT:
                    add_mix(i + 1)
                dve.wait_ge(sem("h2_tr"), i + 1)
                if i >= 2:
                    dve.wait_ge(sem("route_mm"), i - 1)
                dve.tensor_copy(h2T[i % 2][:, 4:8], bank(5).rearrange("p (k t) -> p k t", t=P)).then_inc(sem("h2T_dve"), 1)

            three = lambda v: v.rearrange("p (i e) -> p i e", e=NE)
            L, pr, score, rank, sel, mask, pm, comb, sl, hit, tmp, tmp2 = rt
            st, mx, gs, gr, tot_, cnt, nt_, end_, base_, s1, s2, s3 = rs_
            dve.wait_ge(sem("route_mm"), NT)
            link(dve.tensor_copy(L, bank(6)[:, 0:P]))
            link(dve.tensor_reduce(mx[:, 0:NT], three(L), AX_X, ALU.max))
            dve.tensor_tensor(three(L), three(L), b3(mx[:, 0:NT], NE), ALU.subtract).then_inc(step("rt_sub"), 1)
            dve.wait_ge(step("rt_exp"), nth("rt_exp"))
            link(dve.tensor_reduce(st[:, 0:NT], three(pr), AX_X, ALU.add))
            link(dve.reciprocal(st[:, 0:NT], st[:, 0:NT]))
            link(dve.tensor_tensor(three(pr), three(pr), b3(st[:, 0:NT], NE), ALU.mult))

            def ranks(v, r, g):
                n = v.shape[1]
                link(dve.tensor_copy(r, cst[:, C_RANK:C_RANK + 4].unsqueeze(1).to_broadcast([P, n, 4])))
                for d in range(1, 4):
                    w = g[:, :, 0:4 - d]
                    link(dve.tensor_tensor(w, v[:, :, 0:4 - d], v[:, :, d:4], ALU.is_ge))
                    link(dve.tensor_tensor(r[:, :, d:4], r[:, :, d:4], w, ALU.add))
                    link(dve.tensor_tensor(r[:, :, 0:4 - d], r[:, :, 0:4 - d], w, ALU.subtract))

            four = lambda v: v.rearrange("p (n x) -> p n x", x=PG)
            ranks(four(pr), four(rank), four(tmp))
            link(dve.tensor_scalar(sel, rank, 2.0, None, ALU.is_lt))
            link(dve.tensor_tensor(tmp, pr, sel, ALU.mult))
            link(dve.tensor_reduce(gs, four(tmp), AX_X, ALU.add))
            ranks(four(gs), four(gr), four(s1))
            link(dve.tensor_scalar(gr, gr, 1.0, None, ALU.is_lt))
            dve.tensor_tensor(four(mask), four(sel), b3(gr, PG), ALU.mult).then_inc(step("chosen"), 1)
            dve.wait_ge(step("chosen"), nth("chosen"))
            link(dve.tensor_tensor(pm, pr, mask, ALU.mult))
            link(dve.tensor_reduce(st[:, 0:NT], three(pm), AX_X, ALU.add))
            link(dve.reciprocal(st[:, 0:NT], st[:, 0:NT]))
            link(dve.tensor_tensor(three(comb), three(pm), b3(st[:, 0:NT], NE), ALU.mult))
            dve.wait_ge(step("count_mm"), nth("count_mm"))
            before, total = three(bank(7)[:, 0:P]), three(bank(7)[:, P:2 * P])
            link(dve.memset(three(tmp)[:, 0], 0.0))
            for i in range(1, NT):
                link(dve.tensor_tensor(three(tmp)[:, i], three(tmp)[:, i - 1], total[:, i - 1], ALU.add))
            cnt = cnt[:, 0:NE]
            link(dve.tensor_tensor(cnt, three(tmp)[:, NT - 1], total[:, NT - 1], ALU.add))
            link(dve.tensor_tensor(three(sl), before, three(tmp), ALU.add))
            link(dve.tensor_tensor(thr, b3(cnt, NT), cst[:, C_THR:C_THR + 8].unsqueeze(1).to_broadcast([P, NE, NT]), ALU.is_gt))
            nt_, end_, base_ = nt_[:, 0:NE], end_[:, 0:NE], base_[:, 0:NE]
            link(dve.tensor_reduce(nt_, thr, AX_X, ALU.add))
            link(dve.tensor_tensor_scan(out=end_, data0=ones[:, 0:NE], data1=nt_, initial=0.0, op0=ALU.mult, op1=ALU.add))
            link(dve.tensor_tensor(base_, end_, nt_, ALU.subtract))
            link(dve.tensor_scalar(base_, base_, float(P), 1.0, ALU.mult, ALU.add))
            link(dve.tensor_tensor(three(sl), three(sl), base_.unsqueeze(1).to_broadcast([P, NT, NE]), ALU.add))
            link(dve.tensor_tensor(sl, sl, mask, ALU.mult))
            s1, s2 = s1[:, 0:NT], s2[:, 0:NT]
            link(dve.tensor_reduce(s2, three(sl), AX_X, ALU.max))
            link(dve.tensor_reduce(s1, three(sl), AX_X, ALU.add))
            link(dve.tensor_tensor(s1, s1, s2, ALU.subtract))
            for v, wgt, slot in ((s1, wgt_a, slot_a), (s2, wgt_b, slot_b)):
                link(dve.tensor_tensor(three(hit), three(sl), b3(v, NE), ALU.is_equal))
                link(dve.tensor_tensor(hit, hit, comb, ALU.mult))
                link(dve.tensor_reduce(wgt, three(hit), AX_X, ALU.add))
                link(dve.tensor_scalar(v, v, -1.0, None, ALU.add))
                dve.tensor_copy(slot, v).then_inc(sem("slot_ready"), 1)
            link(dve.tensor_tensor(til, b3(cst[:, C_J:C_J + 32], NE), end_.unsqueeze(1).to_broadcast([P, 32, NE]), ALU.is_ge))
            link(dve.tensor_reduce(s3, til, AX_X, ALU.add))
            link(dve.tensor_scalar(s3, s3, float(NE - 1), None, ALU.min))
            dve.tensor_copy(expert_i, s3).then_inc(step("expert_ready"), 1)

            def take_rows(t, j):
                dve.wait_ge(sem("moe_T"), t + 1)
                if not (isinstance(t, int) and t < 2):
                    dve.wait_ge(sem("moe_gu"), t - 1)
                dve.tensor_copy(rowT[j % 2][:, 4:8], bank(3).rearrange("p (k t) -> p k t", t=P)).then_inc(sem("rowT_dve"), 1)

            def take_answer(t, j, r):
                dve.wait_ge(sem("moe_dn"), t + 1)
                if not (isinstance(t, int) and t < 2):
                    dve.wait_ge(sem(f"y_out{j % 2}"), 32 * r + 16 * (j // 2))
                dve.tensor_copy(answer[j % 2][:, 512:1024], bank(6)).then_inc(sem("y_dve"), 1)

            def hidden(t, j, r):
                dve.wait_ge(sem("silu_ready"), t + 1)
                if not (isinstance(t, int) and t < 2):
                    dve.wait_ge(sem("moe_HT"), t - 1)
                dve.tensor_tensor(hid[j % 2], silu[j % 2], bank(j % 2)[:, FF:2 * FF], ALU.mult).then_inc(sem("hid_ready"), 1)
                if not (isinstance(t, int) and t == 0):
                    take_answer(t - 1, (j - 1) % 4, r if j else r - 1)
                if not (isinstance(t, int) and t == TILES - 1):
                    take_rows(t + 1, (j + 1) % 4)
                dve.wait_ge(sem("moe_HT"), t + 1)
                if not (isinstance(t, int) and t < 2):
                    dve.wait_ge(sem("moe_dn"), t - 1)
                dve.tensor_copy(hidT[j % 2], bank(4)[:, 0:FF].rearrange("p (k t) -> p k t", t=P)).then_inc(sem("hidT_ready"), 1)

            take_rows(0, 0)
            each_tile(dve, hidden)
            take_answer(TILES - 1, (TILES - 1) % 4, TILES // 4)

            dve.wait_ge(sem("last_in"), 32)
            for i in range(NT + 1):
                if i < NT:
                    b = i % NY
                    dve.wait_ge(sem("ya_scaled"), i + 1)
                    dve.wait_ge(sem(f"yb_in{b}"), 16 * (i // NY + 1))
                    link(dve.scalar_tensor_tensor(out=y_a[b], in0=y_b[b], scalar=wgt_b[:, i:i + 1], in1=y_a[b], op0=ALU.mult, op1=ALU.add))
                    link(dve.tensor_tensor(y_a[b], y_a[b], gfb, ALU.mult))
                    dve.tensor_tensor(x2[:, i], x2[:, i], y_a[b], ALU.add).then_inc(sem("x3_ready"), 1)
                if i >= 1:
                    c = i - 1
                    dve.wait_ge(sem("rstd3"), c + 1)
                    if c >= 2:
                        dve.wait_ge(sem(f"out{c % 2}"), 16 * (c // 2))
                    dve.scalar_tensor_tensor(out=fin[c % 2], in0=x2[:, c], scalar=rstd3[:, c:c + 1], in1=fnw, op0=ALU.mult, op1=ALU.mult).then_inc(sem("fin_ready"), 1)

        @block.tensor
        def _(pe):
            def modulation(n):
                pe.wait_ge(sem(f"ada_in{n % 2}"), 16 * (n // 2 + 1))
                if n >= 4:
                    pe.wait_ge(sem("mod_row"), n - 3)
                for k in range(KD):
                    mm = pe.matmul(bank(n % 4)[0:1], cact[:, k:k + 1], ada_ring[n % 2][:, k], start=(k == 0), stop=(k == KD - 1))
                mm.then_inc(sem("ada_mm"), 1)

            pe.wait_ge(step("cact"), nth("cact"))
            modulation(0)
            modulation(1)
            pe.wait_ge(sem("const_in"), 32)
            modulation(2)
            modulation(3)
            pe.wait_ge(step("s5_BA"), nth("s5_BA"))
            pe.wait_ge(step("s5_CA"), nth("s5_CA"))
            for m in range(S5_M):
                for a in range(2):
                    mm = pe.transpose(psum[:, 2048 + (2 * m + a) * P:2048 + (2 * m + a + 1) * P],
                                      s5_BA[:, a, m].rearrange("p s c -> p (s c)"), ident)
            mm.then_inc(step("s5_W_tr"), 1)
            modulation(4)
            modulation(5)
            pe.wait_ge(sem("s5_W"), 4)
            for par in range(2):
                h = slice(64 * par, 64 * par + 64)
                for m in range(S5_M):
                    o = psum[0:S5_C, 2048 + 1024 * par + m * P:2048 + 1024 * par + (m + 1) * P]
                    for a in range(2):
                        mm = pe.matmul(o, s5_bb[h, a, m], s5_CA[h, a, m, 0:8].rearrange("p n c -> p (n c)"),
                                       start=(a == 0), stop=(a == 1))
            mm.then_inc(step("s5_kern"), 1)
            for n in range(6, 12):
                modulation(n)
            pe.wait_ge(step("kz_full"), nth("kz_full"))
            for i in range(NT):
                pe.wait_ge(sem("h_add"), i + 1)
                if i >= 2:
                    pe.wait_ge(sem("hT_act"), i - 1)
                    pe.wait_ge(sem("hT_dve"), i - 1)
                for k in range(KD):
                    mm = pe.transpose(psum[:, 2048 + 1024 * (i % 2) + k * P:2048 + 1024 * (i % 2) + (k + 1) * P],
                                      x_sb[:, i, k * P:(k + 1) * P], ident)
                mm.then_inc(sem("h_tr"), 1)

            def project(name):
                for u in unit_range(name):
                    g, where = UNITS[u]
                    _, _, w, tok, _ = GROUPS[g]
                    ring = win_ring[g % 2]
                    if u == unit_range(name)[0]:
                        pe.wait_ge(sem(f"win_in{g % 2}"), 16 * (g // 2 + 1))
                    if u >= WIN_BANKS:
                        for e in ("act", "dve"):
                            if evacuated(e, u - WIN_BANKS):
                                pe.wait_ge(sem(f"ev_{e}"), evacuated(e, u - WIN_BANKS))
                    for k in range(KD):
                        if name == "su":
                            mm = pe.matmul(bank(u % WIN_BANKS)[:, 0:w], hT[:, k, where::S5_L], ring[:, k, 0:w], start=(k == 0), stop=(k == KD - 1))
                        elif tok:
                            mm = pe.matmul(bank(u % WIN_BANKS)[:, 0:w], hT[:, k, where * P:(where + 1) * P], ring[:, k, 0:w],
                                           start=(k == 0), stop=(k == KD - 1))
                        else:
                            m, h = where
                            mm = pe.matmul(bank(u % WIN_BANKS), ring[:, k, m * P:(m + 1) * P], hT[:, k, 512 * h:512 * h + 512],
                                           start=(k == 0), stop=(k == KD - 1))
                    mm.then_inc(sem("win_mm"), 1)

            pe.wait_ge(sem("hT_act"), NT)
            pe.wait_ge(sem("hT_dve"), NT)
            pe.wait_ge(sem("mod_row"), 12)
            project("su")
            pe.wait_ge(sem("ev_dve"), evacuated("dve", NT - 1))
            for g in range(S5_G):
                mm = pe.transpose(psum[:, 2048 + g * P:2048 + (g + 1) * P], s5_Z[:, g].rearrange("p s c -> p (s c)"), ident)
            mm.then_inc(step("s5_U_tr"), 1)
            project("hq")
            pe.wait_ge(sem("s5_U"), 4)
            for a in range(2):
                for g in range(S5_G):
                    m, h = g // 2, 64 * (g % 2)
                    mm = pe.matmul(psum[h:h + 64, 2048 + 1024 * a + m * P:2048 + 1024 * a + (m + 1) * P],
                                   s5_W[:, m, a, h:h + 64], s5_U[:, g], start=True, stop=True)
            mm.then_inc(step("s5_V_mm"), 1)
            project("hi")
            project("hg")
            pe.wait_ge(sem("s5_X"), 2)
            pe.wait_ge(sem("s5_T_in"), 16 * S5_L)
            for par in range(2):
                h = slice(64 * par, 64 * par + 64)
                for m in range(S5_M):
                    o = psum[:, 2048 + 1024 * par + m * P:2048 + 1024 * par + (m + 1) * P]
                    pe.matmul(o, s5_U[:, 2 * m + par], s5_T[:, 2 * m + par], start=True, stop=False)
                    for a in range(2):
                        mm = pe.matmul(o, s5_X[a][h, m], s5_CA[h, a, m, 1:9].rearrange("p n c -> p (n c)"), start=False, stop=(a == 1))
            mm.then_inc(step("s5_y_mm"), 1)
            project("hf")
            pe.wait_ge(sem("s5_gelu"), 4)
            for c in range(2):
                for st in range(S5_L):
                    mm = pe.transpose(psum[:, 2048 + (8 * c + st) * P:2048 + (8 * c + st + 1) * P], s5_y[:, st, c * P:(c + 1) * P], ident)
            mm.then_inc(step("s5_y_tr"), 1)
            project("fv")
            pe.wait_ge(sem("s5_yT"), 4)
            pe.wait_ge(sem("glu_in"), 16)
            for st in range(S5_L):
                o = psum[:, 2048 + S5_W * st:2048 + S5_W * (st + 1)]
                pe.matmul(o, ones[0:1], glu_b, start=True, stop=False)
                for c in range(2):
                    mm = pe.matmul(o, s5_yT[:, c, st], glu_w[:, c], start=False, stop=(c == 1))
            mm.then_inc(step("s5_glu_mm"), 1)
            project("fq")
            pe.wait_ge(step("s5_o"), nth("s5_o"))
            for c in range(2):
                for st in range(S5_L):
                    mm = pe.transpose(psum[:, 2048 + (8 * c + st) * P:2048 + (8 * c + st + 1) * P], s5_y[:, st, c * P:(c + 1) * P], ident)
            mm.then_inc(step("s5_o_tr"), 1)
            project("fk")

            def level_scores(rnd, l):
                for h in range(HG_H):
                    c = (rnd * (1 + n_lev) + l) * HG_H + h
                    if c >= 4:
                        pe.wait_ge(sem("hg_taken"), c - 3)
                    hs, m = slice(64 * (h % 2), 64 * (h % 2) + 64), h // 2
                    for n in range(4):
                        if l == 0:
                            ts = slice((4 * rnd + n) * P, (4 * rnd + n + 1) * P)
                            k_, q_ = hk[hs, m, ts], hq[hs, m, ts]
                        else:
                            k_ = q_ = lev[(rnd * n_lev + l - 1) % 2][hs, m, n * P:(n + 1) * P]
                        mm = pe.matmul(bank(c % 4)[:, n * P:(n + 1) * P], k_, q_, start=True, stop=True)
                    mm.then_inc(sem("hg_mm"), 1)

            pe.wait_ge(sem("ev_dve"), evacuated("dve", len(UNITS) - 1))
            pe.wait_ge(sem("ev_act"), evacuated("act", len(UNITS) - 1))
            pe.wait_ge(sem("s5_done"), 4)
            pe.wait_ge(step("hk_ready"), nth("hk_ready"))
            for rnd in range(2):
                level_scores(rnd, 0)
                pe.wait_ge(step("ke_ready"), nth("ke_ready"))
                if rnd:
                    pe.wait_ge(sem("hg_o_taken"), 4 * rnd)
                for n in range(4):
                    for m in range(HG_M):
                        mm = pe.transpose(bank(4 + n)[:, m * P:(m + 1) * P], ke[:, m, (4 * rnd + n) * P:(4 * rnd + n + 1) * P], ident)
                    mm.then_inc(sem("ke_tr"), 1)
                for n in range(4):
                    if 4 * rnd + n == NT - 1:
                        break
                    pe.wait_ge(sem("keT_ready"), 4 * rnd + 4 if n == 0 else 4 * rnd + n + 1)
                    for h in range(HG_H):
                        p0, m = 64 * (h % 2), h // 2
                        mm = pe.matmul(psum[p0:p0 + 64, 2048 + 512 * (n // 2) + 192 * (n % 2) + 64 * m:2048 + 512 * (n // 2) + 192 * (n % 2) + 64 * m + 64],
                                       keT[4 * rnd + n][:, 64 * h:64 * h + 64], hv[:, 4 * rnd + n, 64 * h:64 * h + 64], start=True, stop=True)
                    mm.then_inc(sem("dS_mm"), 1)
                for l in range(1, 1 + n_lev):
                    pe.wait_ge(sem("lev_q"), rnd * n_lev + l)
                    pe.wait_ge(sem("lev_k"), rnd * n_lev + l)
                    level_scores(rnd, l)
                pe.wait_ge(sem("hg_taken"), (rnd + 1) * (1 + n_lev) * HG_H)
                pe.wait_ge(sem("hg_S"), min(4 * rnd + 4, NT - 1))
                pe.wait_ge(step("qe_ready"), nth("qe_ready"))
                for h in [0, 2, 4, 1, 3, 5]:
                    hs, m = slice(64 * (h % 2), 64 * (h % 2) + 64), h // 2
                    for n in range(4):
                        o0 = 2048 + 1024 * (h % 2) + 512 * (n // 2) + 192 * (n % 2) + 64 * m
                        first = 4 * rnd + n == 0
                        mm = pe.matmul(psum[:, o0:o0 + 64], sT[:, h, n], hv[:, 4 * rnd + n, 64 * h:64 * h + 64], start=True, stop=first)
                        if not first:
                            mm = pe.matmul(psum[:, o0:o0 + 64], qe[hs, m, (4 * rnd + n) * P:(4 * rnd + n + 1) * P],
                                           hg_S[hs, 4 * rnd + n - 1, 64 * m:64 * m + 64], start=False, stop=True)
                mm.then_inc(sem("hg_o_mm"), 1)
            for n in range(NT):
                pe.wait_ge(sem("hg_gated"), n // 4 + 1)
                pe.wait_ge(sem("hg_o_taken"), 8)
                if n >= 4:
                    pe.wait_ge(sem("cHg_ready"), n - 3)
                for m in range(HG_M):
                    mm = pe.transpose(bank(4 + n % 4)[:, m * P:(m + 1) * P], hgate[:, n, m * P:(m + 1) * P], ident)
                mm.then_inc(sem("hg_o_tr"), 1)

            pe.wait_ge(sem("cHg_ready"), NT)
            pe.wait_ge(sem("flog"), 2)
            for i in range(NT):
                mm = pe.transpose(psum[0:FOX_H, 2048 + i * P:2048 + (i + 1) * P], flog[:, i * FOX_H:(i + 1) * FOX_H], ident)
            mm.then_inc(step("f_tr"), 1)
            pe.wait_ge(sem("mask16"), 2)
            pe.wait_ge(sem("aug_in"), 16 * 2 * FOX_H)

            def logits(u):
                i, h = units[u]
                if u >= 2:
                    pe.wait_ge(sem("f_exp"), u - 1)
                w = (i + 1) * P
                s0 = 1024 * (u % 2)
                for c in range(0, w, 512):
                    e = min(w, c + 512)
                    mm = pe.matmul(psum[:, s0 + c:s0 + e], qaug[0:66, h, i * P:(i + 1) * P], kaug[0:66, h, c:e], start=True, stop=(e < w))
                pe.matmul(psum[:, s0 + w - P:s0 + w], ident16[:], neg16[:], start=False, stop=True).then_inc(sem("f_qk"), 1)

            def turn(u):
                i, h = units[u]
                pe.wait_ge(sem("f_exp"), u + 1)
                if u >= 1:
                    pe.wait_ge(sem("fT_dve"), u)
                    pe.wait_ge(sem("fT_act"), sum(units[v][0] >= 4 for v in range(u))) if units[u - 1][0] >= 4 else None
                for kb in range(i + 1):
                    mm = pe.transpose(psum[:, 2048 + kb * P:2048 + (kb + 1) * P], prob[u % 2][:, kb * P:(kb + 1) * P], ident)
                mm.then_inc(sem("f_T"), 1)

            def values(u):
                i, h = units[u]
                pe.wait_ge(sem("fT_dve"), u + 1)
                if i >= 4:
                    pe.wait_ge(sem("fT_act"), sum(units[v][0] >= 4 for v in range(u + 1)))
                if h == 0 and i >= 2:
                    pe.wait_ge(sem("cFox_ready"), i - 1)
                for kb in range(i + 1):
                    mm = pe.matmul(bank(6 + i % 2)[:, h * FOX_D:(h + 1) * FOX_D], probT[u % 2][:, kb], fv[:, kb, h * FOX_D:(h + 1) * FOX_D],
                                   start=(kb == 0), stop=(kb == i))
                mm.then_inc(sem("f_pv"), 1)

            def fox_out(i):
                pe.wait_ge(sem("fo_ready"), i + 1)
                for m in range(3):
                    mm = pe.transpose(bank(6 + i % 2)[:, m * P:(m + 1) * P], fo[i % 2][:, m * P:(m + 1) * P], ident)
                mm.then_inc(sem("fo_tr"), 1)

            logits(0)
            for u in range(len(units)):
                if u + 1 < len(units):
                    logits(u + 1)
                turn(u)
                if u >= 1:
                    values(u - 1)
                i, h = units[u]
                if i >= 1 and h == 4:
                    fox_out(i - 1)
            values(len(units) - 1)
            fox_out(NT - 1)

            pe.wait_ge(sem("cFox_ready"), NT)
            pe.wait_ge(step("w_scaled"), nth("w_scaled"))

            def mix(i):
                if i >= 2:
                    pe.wait_ge(sem("mix_taken"), i - 1)
                for n in range(2):
                    for k in range(KD):
                        mm = pe.matmul(bank(2 * (i % 2) + n), branch[k][:, i * P:(i + 1) * P], w_out[:, k, 512 * n:512 * n + 512],
                                       start=(k == 0), stop=(k == KD - 1))
                mm.then_inc(sem("mix_mm"), 1)

            def turn_h2(i):
                pe.wait_ge(sem("h2_ready"), i + 1)
                if i >= 1:
                    pe.wait_ge(sem("h2T_act"), i)
                    pe.wait_ge(sem("h2T_dve"), i)
                for k in range(KD):
                    mm = pe.transpose(psum[:, 2048 + k * P:2048 + (k + 1) * P], h2[i % 2][:, k * P:(k + 1) * P], ident)
                mm.then_inc(sem("h2_tr"), 1)

            def route(i):
                pe.wait_ge(sem("h2T_act"), i + 1)
                pe.wait_ge(sem("h2T_dve"), i + 1)
                o = bank(6)[:, NE * i:NE * (i + 1)]
                pe.matmul(o, ones[0:1], router_b, start=True, stop=False)
                for k in range(KD):
                    mm = pe.matmul(o, h2T[i % 2][:, k], router_w[:, k], start=False, stop=(k == KD - 1))
                mm.then_inc(sem("route_mm"), 1)

            mix(0)
            for i in range(NT):
                if i + 1 < NT:
                    mix(i + 1)
                turn_h2(i)
                route(i)
            pe.wait_ge(step("chosen"), nth("chosen"))
            pe.matmul(bank(7)[:, 0:P], cst[:, C_LT:C_LT + P], rt[5], start=True, stop=True)
            pe.matmul(bank(7)[:, P:2 * P], ones, rt[5], start=True, stop=True).then_inc(step("count_mm"), 1)

            def turn_rows(t, j, r):
                pe.wait_ge(sem(f"row_in{j}"), 16 * r + 16)
                for k in range(KD):
                    mm = pe.transpose(psum[:, 1024 + k * P:1024 + (k + 1) * P], rows[j][:, k * P:(k + 1) * P], ident)
                mm.then_inc(sem("moe_T"), 1)

            def down(t, j, r):
                pe.wait_ge(sem("hidT_ready"), t + 1)
                pe.wait_ge(sem(f"dn_in{j}"), 16 * r + 16)
                if not (isinstance(t, int) and t == 0):
                    pe.wait_ge(sem("y_act"), t)
                    pe.wait_ge(sem("y_dve"), t)
                for n in range(2):
                    for k in range(2):
                        mm = pe.matmul(bank(5 + n), hidT[j % 2][:, k], wdn[j][:, k, 512 * n:512 * n + 512], start=(k == 0), stop=(k == 1))
                mm.then_inc(sem("moe_dn"), 1)

            def expert(t, j, r):
                pe.wait_ge(sem("rowT_act"), t + 1)
                pe.wait_ge(sem("rowT_dve"), t + 1)
                if not (isinstance(t, int) and t < 2):
                    pe.wait_ge(sem("hid_ready"), t - 1)
                pe.wait_ge(sem(f"gu_in{j}"), 16 * r + 16)
                for k in range(KD):
                    mm = pe.matmul(bank(j % 2), rowT[j % 2][:, k], wgu[j][:, k], start=(k == 0), stop=(k == KD - 1))
                mm.then_inc(sem("moe_gu"), 1)
                if not (isinstance(t, int) and t == 0):
                    down(t - 1, (j - 1) % 4, r if j else r - 1)
                if not (isinstance(t, int) and t == TILES - 1):
                    turn_rows(t + 1, (j + 1) % 4, r if j < 3 else r + 1)
                pe.wait_ge(sem("hid_ready"), t + 1)
                if not (isinstance(t, int) and t == 0):
                    pe.wait_ge(sem("hidT_ready"), t)
                for k in range(2):
                    mm = pe.transpose(bank(4)[:, k * P:(k + 1) * P], hid[j % 2][:, k * P:(k + 1) * P], ident)
                mm.then_inc(sem("moe_HT"), 1)

            turn_rows(0, 0, 0)
            each_tile(pe, expert)
            down(TILES - 1, (TILES - 1) % 4, TILES // 4)


def lay_out(a):
    def pairs(v):
        v = v.reshape(S5_M, 2, S5_P, -1).transpose(1, 2, 0, 3)
        return v.reshape(P, -1)

    def blocks(v):
        return v.reshape(-1, P, v.size // v.shape[0]).transpose(1, 0, 2).reshape(P, -1)

    rows = lambda v: np.broadcast_to(v.reshape(1, -1), (P, v.size))
    d = np.zeros((P, S5_G), np.float32)
    d[0:S5_C] = a["s5_d"][0].T
    dt = np.broadcast_to(a["s5_log_dt"][0][:, None], (S5_G, S5_P))
    w = {n: a[n] for n in ("x", "ada_b")}
    w["ada_w"] = a["ada_w"][0].reshape(KD, P, ADA // ADA_N, ADA_N).transpose(2, 1, 0, 3)
    w["w_in"] = a["w_in"][0].reshape(KD, P, N_IN).transpose(1, 0, 2)
    w["c_col"] = blocks(a["c"][0])
    w["s5_par"] = np.concatenate([pairs(a["s5_a_re"][0]), pairs(a["s5_a_im"][0]), pairs(dt), d,
                                  pairs(a["s5_b_re"][0]), pairs(a["s5_b_im"][0]),
                                  pairs(a["s5_c_re"][0].transpose(0, 2, 1)), pairs(a["s5_c_im"][0].transpose(0, 2, 1))], 1)
    w["late"] = np.concatenate([rows(a["fox_f_bias"][0]),
                                blocks(np.concatenate([a["branch_norm_fox"][0], a["branch_norm_s5"][0],
                                                       np.tile(a["hgrn_norm_w"][0], HG_H)])),
                                blocks(a["router_w"]), rows(a["router_b"])], 1)
    w["glu"] = np.concatenate([blocks(a["s5_glu_w"][0]), rows(a["s5_glu_b"][0])], 1)
    w["w_out"] = blocks(a["w_out"][0])
    w["norms"] = np.concatenate([a["norm_mix_w"], a["norm_ffn_w"], a["final_norm_w"][None]])
    w["gate_up"] = np.concatenate([a["moe_w_gate"][0], a["moe_w_up"][0]], 2).reshape(NE, KD, P, 2 * FF).transpose(0, 2, 1, 3)
    w["down"] = a["moe_w_down"][0].reshape(NE, 2, P, D).transpose(0, 2, 1, 3)
    w["cst"], w["lmask"] = shape_constants()
    return {f"in_{n}": np.ascontiguousarray(v) for n, v in w.items()}


def kernel(**inputs):
    import concourse.bacc as _bacc
    from concourse.bass_utils import run_bass_kernel_spmd as _run

    nc = _bacc.Bacc("TRN2", target_bir_lowering=False, num_devices=1)
    arrays = lay_out(inputs)
    A = {n[3:]: nc.dram_tensor(n, a.shape, mybir.dt.from_np(a.dtype), kind="ExternalInput").ap() for n, a in arrays.items()}
    out = nc.dram_tensor("out", (1, T, D), F32, kind="ExternalOutput").ap()
    hybrid_trunk_layer(nc, A, out)
    r = _run(nc, [arrays], core_ids=[0])
    return r.results[0]["out"]
```

```python
from contextlib import ExitStack

import numpy as np
import concourse.bass as bass
from concourse import mybir

ALU = mybir.AluOpType
ACT = mybir.ActivationFunctionType
F32 = mybir.dt.float32
I32 = mybir.dt.int32
BF16 = mybir.dt.bfloat16
AX_X = mybir.AxisListType.X

P = 128
D = 1024
T = 1024
KD = D // P
NT = T // P
EPS = 1e-6
FOX_H, FOX_D = 6, 64
FOX_W = FOX_H * FOX_D
S5_G, S5_C, S5_P = 16, 16, 64
S5_W = S5_G * S5_C
S5_M = S5_G // 2
S5_L = 8
S5_J = T // S5_L
HG_H, HG_D = 6, 64
HG_W = HG_H * HG_D
HG_M = HG_W // P
NE, NG, PG = 16, 4, 4
FF = 256
ADA = 6 * D
ADA_N = 512
TILES = (2 * T + NE * (P - 1)) // P
SLOTS = TILES * P
TWO_PI = 6.2831850
ROUND = 12582912.0

O_FQ, O_FK, O_FV = 0, FOX_W, 2 * FOX_W
O_SU = 3 * FOX_W + FOX_H
O_HQ = O_SU + S5_W
O_HF, O_HI, O_HG = O_HQ + HG_W, O_HQ + 2 * HG_W, O_HQ + 3 * HG_W
N_IN = O_HQ + 4 * HG_W
VW = FOX_W + FOX_H

GROUPS = [
    ("su", O_SU, S5_W, True, "dve"),
    ("hq", O_HQ, HG_W, False, "act"),
    ("hi", O_HI, HG_W, True, "dve"),
    ("hg", O_HG, HG_W, True, "act"),
    ("hf", O_HF, HG_W, False, "dve"),
    ("fv", O_FV, VW, True, "dve"),
    ("fq", O_FQ, FOX_W, False, "act"),
    ("fk", O_FK, FOX_W, False, "dve"),
]
UNITS = []
for gi, (_, _, _, tok, _) in enumerate(GROUPS):
    UNITS += [(gi, u) for u in range(NT)] if tok else [(gi, (m, h)) for m in range(3) for h in range(2)]
WIN_BANKS = 4
LEVELS = [64, 32, 16, 8, 4, 2, 1]


def evacuated(engine, u):
    return sum(GROUPS[g][4] == engine for g, _ in UNITS[:u + 1])


STEPS = {
    "pe": "s5_W_tr s5_kern s5_U_tr s5_V_mm s5_y_mm s5_y_tr s5_glu_mm s5_o_tr f_tr count_mm list_mm".split(),
    "act": "cact s5_dt s5_gate hk_ready e_kb efin e_b w_scaled rt_exp".split(),
    "dve": "s5_ph s5_rot s5_BA s5_CA kz_full sssq s5_o ke_ready cum_ready qe_ready rt_sub chosen expert_ready picks tok_set".split(),
    "pool": "mhalf_set kz_zero rstd_x srstd aug_zero d_kb a2_mul a2_ready".split(),
}


def unit_range(name):
    return [u for u, (g, _) in enumerate(UNITS) if GROUPS[g][0] == name]


C_ID, C_ONE, C_LT, C_NEG = 0, P, 2 * P, 3 * P
C_J = 4 * P
C_POW = 5 * P
C_THR = C_POW + 17
C_RANK = C_THR + 8
C_TOK = C_RANK + 4
C_F = C_TOK + NT
S5_PAR = 3 * S5_M + S5_G + 4 * S5_M * S5_C


def shape_constants():
    p = np.arange(P)
    c = np.zeros((P, C_F), np.float32)
    c[:, C_ID:C_ID + P] = np.eye(P)
    c[:, C_ONE:C_ONE + P] = 1.0
    c[:, C_LT:C_LT + P] = p[:, None] < p[None, :]
    c[:, C_NEG:C_NEG + P] = np.where(p[None, :] > p[:, None], -1e30, 0.0)
    c[:, C_J:C_J + P] = p[None, :]
    c[:, C_POW:C_POW + 17] = np.r_[np.arange(9), np.arange(7, -1, -1)]
    c[:, C_THR:C_THR + 8] = 128.0 * np.arange(8)
    c[:, C_RANK:C_RANK + 4] = [3, 2, 1, 0]
    c[:, C_TOK:C_TOK + NT] = p[:, None] + P * np.arange(NT)
    m = np.zeros((P, 1 + len(LEVELS), P), np.int32)
    m[:, 0] = np.eye(P)
    s, t = p[:, None], p[None, :]
    for n, half in enumerate(LEVELS):
        m[:, 1 + n] = (s // (2 * half) == t // (2 * half)) & (s % (2 * half) < half) & (t % (2 * half) >= half)
    return c, m.reshape(P, -1)


def hybrid_trunk_layer(nc, A, out):
    ctx = ExitStack()
    with ctx:
        def sb(name, cols, dt=F32):
            return ctx.enter_context(nc.sbuf_tensor(name, [P, cols], dt))

        sems = {}

        def sem(name):
            if name not in sems:
                sems[name] = ctx.enter_context(nc.semaphore(name))
            return sems[name]

        def step(name):
            return sem(next(f"{e}_step" for e in STEPS if name in STEPS[e]))

        def nth(name):
            return next(STEPS[e].index(name) + 1 for e in STEPS if name in STEPS[e])

        def dram(name, shape, dt=F32):
            return nc.dram_tensor(name, shape, dt, kind="Internal").ap()

        mod_d = dram("mod_d", (6, D))
        kern_d = dram("kern_d", (S5_C, S5_G, 2 * P))
        h2_d = dram("h2_d", (T, D))
        y_d = dram("y_d", (SLOTS, D))

        psum = ctx.enter_context(nc.psum_tensor("psum", [P, 4096], F32))

        def bank(b, n=1):
            return psum[:, 512 * b:512 * (b + n)]

        cst = sb("cst", C_F)
        lmask = sb("lmask", (1 + len(LEVELS)) * P, I32)
        ident, ones = cst[:, C_ID:C_ID + P], cst[:, C_ONE:C_ONE + P]
        masks = lmask[:].rearrange("p (l t) -> p l t", t=P)
        small = sb("small", 780)
        ident16, neg16 = sb("ident16", P, BF16), sb("neg16", P, BF16)
        idle16 = lmask[:, 0:256].bitcast(BF16)
        at = [0]

        def little(n, dt=F32):
            v = small[:, at[0]:at[0] + n]
            at[0] += n
            return v if dt == F32 else v.bitcast(dt)

        cact = little(KD)
        ssq, rstd = little(NT), little(NT)
        mhalf = little(NT * HG_H)
        late = little(FOX_H + KD + KD * NE + NE)
        fbias = late[:, 0:FOX_H]
        wrow = late[:, FOX_H:FOX_H + KD]
        router_w = late[:, FOX_H + KD:FOX_H + KD + KD * NE].rearrange("p (k e) -> p k e", e=NE)
        router_b = late[0:1, FOX_H + KD + KD * NE:]
        hg_ss, hg_r, rowsum = little(NT * HG_H), little(NT * HG_H), little(NT * FOX_H)
        negmax, rinv = hg_ss, hg_r
        fssq, frstd, sssq, srstd = little(NT), little(NT), little(NT), little(NT)
        efin = little(HG_M * NT)
        flog, fln = little(NT * FOX_H), little(NT * FOX_H)

        def cut(region, start, *shape):
            n = int(np.prod(shape))
            v = region[:, start:start + n]
            if len(shape) == 1:
                return v
            names = "abcd"[:len(shape)]
            return v.rearrange(f"p ({' '.join(names)}) -> p {' '.join(names)}",
                               **{k: s for k, s in zip(names[1:], shape[1:])})

        ra = sb("region_a", 12288)
        rb = sb("region_b", 8192)
        rc = sb("region_c", 8192)
        rd = sb("region_d", 15360)
        re_ = sb("region_e", 6512)

        hT = cut(rb, 0, KD, T)
        ada_ring = [cut(rc, 4096 * i, KD, ADA_N) for i in range(2)]
        win_ring = [cut(rc, 4096 * i, KD, 512) for i in range(2)]
        x_sb = cut(rd, 0, NT, D)
        mod_row = rd[0:1, 8192:8192 + ADA]
        a1b, b1b, nmw = cut(ra, 0, D), cut(ra, 1024, D), cut(ra, 2048, D)

        hq, hb, hk = cut(rd, 0, HG_M, T), cut(rd, 3072, HG_M, T), cut(rd, 6144, HG_M, T)
        hv, hgate = cut(rd, 9216, NT, HG_W), cut(rd, 12288, NT, HG_W)
        fv = cut(re_, 0, NT, VW)
        cS5 = cut(re_, 3120, 2, T)
        hg_tmp = cut(re_, 5168, T)

        s5_W = cut(ra, 3072, S5_M, 2, P)
        s5_CA = cut(ra, 5120, 2, S5_M, 9, S5_C)
        s5_T = cut(ra, 7424, S5_G, P)
        s5_cos, s5_sin = cut(ra, 9472, S5_M * S5_J), cut(ra, 10496, S5_M * S5_J)
        glu_w = cut(ra, 11520, 2, S5_W)
        glu_b = ra[0:1, 12032:12288]
        s5_R = cut(re_, 5168, S5_M * S5_J)
        kz = rb[0:S5_C, 0:S5_G * 2 * P].rearrange("c (g x) -> c g x", g=S5_G)
        s5_BA = cut(rb, 4096, 2, S5_M, S5_L, S5_C)
        s5_par = rb[:, 6144:6144 + S5_PAR]
        are, aim, dt = [s5_par[:, 8 * i:8 * i + 8] for i in range(3)]
        s5_D = s5_par[0:S5_C, 24:40]
        s5_B = cut(s5_par, 40, 2, S5_M, S5_C)
        s5_Ct = cut(s5_par, 296, 2, S5_M, S5_C)
        s5_bb = cut(rb, 6704, 2, S5_M, S5_C)
        p_mag, p_re, p_im, p_tmp = [cut(rb, 6960 + 136 * i, S5_M, 17) for i in range(4)]
        lr, th, ph8, den, wr, wi, am1, u0, u1 = [cut(re_, 8 * i, S5_M) for i in range(9)]
        s5_tab = [ra[:, 7424:8448], ra[:, 8448:9472]]
        s5_Z = cut(ra, 0, S5_G, S5_L, S5_C)
        s5_V = cut(ra, 0, 2, S5_M * S5_J)
        s5_yT = cut(ra, 0, 2, S5_L, S5_J)
        s5_U = cut(rd, 3072, S5_G, S5_J)
        s5_X = [cut(rd, 5120, S5_M, S5_J), cut(rd, 8192, S5_M, S5_J)]
        s5_t = [cut(rd, 6144, S5_M * S5_J), cut(rd, 7168, S5_M * S5_J)]
        s5_y = cut(rd, 6144, S5_L, S5_W)
        s5_gate = cut(ra, 9472, S5_L, S5_W)
        s5_sq = cut(ra, 7424, S5_L, S5_W)
        qaug, kaug = cut(ra, 0, FOX_H, T), cut(ra, 6144, FOX_H, T)

        qe, ke = cut(rb, 0, HG_M, T), cut(rc, 0, HG_M, T)
        keT = [cut(rb, 6144 + 384 * n, HG_W) if n < 5 else cut(rc, 6144 + 384 * (n - 5), HG_W) for n in range(NT)]
        lev = [cut(rb, 3072 + 1536 * i, HG_M, 512) for i in range(2)]
        lev_q = [[cut(rc, 1024 * m, 2, 512) for m in range(HG_M)],
                 [cut(rb, 6144, 2, 512), cut(rb, 7168, 2, 512), cut(rc, 6144, 2, 512)]]
        sT = cut(rc, 3072, HG_H, 4, P)
        cum, ncum = ra[96:96 + FOX_H, 0:T], ra[96:96 + FOX_H, T:2 * T]
        hg_S = cut(re_, 5168, NT - 1, HG_M * HG_D)
        hg_o = cut(rc, 3072, 4 * HG_H, HG_D)
        hg_sq = cut(rc, 4608, 4 * HG_H, HG_D)
        cHg = cut(rd, 3072, HG_M, T)
        n_lev = len(LEVELS)

        def level_done(c):
            return (c // n_lev * (1 + n_lev) + c % n_lev + 2) * HG_H

        prob = [cut(rd, 6144 + T * i, T) for i in range(2)]
        probT = [cut(rd, 8192 + T * i, NT, P) for i in range(2)]
        fo = [cut(rd, 12288 + FOX_W * i, FOX_W) for i in range(2)]
        fsq = cut(rd, 13056, FOX_W)
        cFox = cut(rd, 0, 3, T)
        units = [(i, h) for i in range(NT) for h in range(FOX_H)]
        x2 = cut(rb, 0, NT, D)
        w_out = cut(rc, 0, KD, D)
        gmb, b2b, a2b, nfw = cut(rd, 10240, D), cut(rd, 11264, D), cut(rd, 13440, D), cut(re_, 5168, D)
        mix_t = [cut(ra, D * i, D) for i in range(2)]
        h2 = [cut(ra, 2048 + D * i, D) for i in range(2)]
        h2T = [cut(ra, 4096 + D * i, KD, P) for i in range(2)]
        sq2 = cut(ra, 6144, D)
        ssq2, rstd2, ssq3, rstd3 = little(NT), little(NT), little(NT), little(NT)
        branch = [cFox[:, 0], cFox[:, 1], cFox[:, 2], cS5[:, 0], cS5[:, 1], cHg[:, 0], cHg[:, 1], cHg[:, 2]]
        rt = [rd[:, 6144 + P * i:6144 + P * (i + 1)] for i in range(12)]
        rs_ = [rd[:, 7680 + 32 * i:7680 + 32 * (i + 1)] for i in range(12)]
        thr = cut(rd, 8192, NE, NT)
        til = cut(rd, 8320, 32, NE)
        slot_a, slot_b = little(NT, I32), little(NT, I32)
        wgt_a, wgt_b = little(NT), little(NT)
        tok_l = little(TILES, I32)
        expert_i = little(32, I32)
        place, number = cut(rd, 0, 2 * NT, P), cut(rd, 2 * NT * P, 2 * NT, 32)
        wgu = [cut(r_, o, KD, 2 * FF) for r_, o in ((ra, 0), (ra, 6144), (rd, 0), (rd, 6144))]
        wdn = [cut(r_, o, 2, D) for r_, o in ((ra, 4096), (ra, 10240), (rd, 4096), (rd, 10240))]
        rows = [cut(rc, D * i, D) for i in range(4)]
        rowT = [cut(rc, 4096 + D * i, KD, P) for i in range(2)]
        answer = [cut(rc, 6144 + D * i, D) for i in range(2)]
        silu = [cut(rd, 12288 + FF * i, FF) for i in range(2)]
        hid = [cut(rd, 12800 + FF * i, FF) for i in range(2)]
        hidT = [cut(rd, 13312 + FF * i, 2, P) for i in range(2)]
        gfb, fnw = cut(re_, 0, D), cut(re_, D, D)
        NY = 6
        y_a, y_b = [cut(ra, 2 * D * i, D) for i in range(NY)], [cut(ra, 2 * D * i + D, D) for i in range(NY)]
        fin = [cut(rd, D * i, D) for i in range(2)]
        sq3 = cut(rd, 2 * D, D)

        def each_tile(eng, body):
            for t in range(4):
                body(t, t, 0)
            with eng.Fori(1, TILES // 4) as i:
                for j in range(4):
                    body(4 * i + j, j, i)
            for t in range(TILES // 4 * 4, TILES):
                body(t, t % 4, t // 4)

        def b3(v, n):
            return v.unsqueeze(2).to_broadcast([v.shape[0], v.shape[1], n])

        block = ctx.enter_context(nc.Block())

        @block.sync
        def _(sp):
            for n in range(ADA // ADA_N):
                if n >= 2:
                    sp.wait_ge(sem("ada_mm"), n - 1)
                sp.dma_start(ada_ring[n % 2], A["ada_w"][n]).then_inc(sem(f"ada_in{n % 2}"), 16)
                if n == 0:
                    sp.dma_start(mod_row, A["ada_b"]).then_inc(sem("ada_b_in"), 16)
                if n == 2:
                    sp.dma_start(x_sb, A["x"][0].rearrange("(i p) d -> p i d", p=P)).then_inc(sem("x_in"), 16)
            for g, (name, o, w, tok, _) in enumerate(GROUPS):
                if g < 2:
                    sp.wait_ge(sem("ada_mm"), ADA // ADA_N - 1 + g)
                else:
                    sp.wait_ge(sem("win_mm"), unit_range(GROUPS[g - 2][0])[-1] + 1)
                sp.dma_start(win_ring[g % 2][:, :, 0:w], A["w_in"][:, :, o:o + w]).then_inc(sem(f"win_in{g % 2}"), 16)

            sp.wait_ge(step("cum_ready"), nth("cum_ready"))
            sp.wait_ge(sem("aug_ones"), 1)
            for h in range(FOX_H):
                sp.dma_start(qaug[64:65, h], cum[h:h + 1]).then_inc(sem("aug_in"), 16)
                sp.dma_start(kaug[65:66, h], ncum[h:h + 1]).then_inc(sem("aug_in"), 16)
            sp.wait_ge(sem("hg_gated"), 2)
            sp.dma_start(rc[:], A["w_out"]).then_inc(sem("w_out_in"), 16)
            sp.dma_start(x2, A["x"][0].rearrange("(i p) d -> p i d", p=P)).then_inc(sem("x2_in"), 16)
            for i in range(NT):
                sp.wait_ge(sem("h2_ready"), i + 1)
                sp.dma_start(h2_d[i * P:(i + 1) * P], h2[i % 2]).then_inc(sem(f"h2_out{i % 2}"), 16)

            sp.wait_ge(step("expert_ready"), nth("expert_ready"))

            def load(t, j, r):
                e = sp.value_load(expert_i[0:1, bass.ds(t, 1)], min_val=0, max_val=NE - 1)
                if isinstance(t, int) and t == 1:
                    sp.wait_ge(sem("row_in0"), 16)
                if isinstance(t, int) and t == 3:
                    sp.wait_ge(sem("weights_set"), 2)
                if not (isinstance(r, int) and r == 0):
                    sp.wait_ge(sem("moe_gu"), 4 * r + j - 3)
                sp.dma_start(wgu[j], A["gate_up"][bass.ds(e, 1)].rearrange("o p k n -> (o p) k n")).then_inc(sem(f"gu_in{j}"), 16)
                if not (isinstance(r, int) and r == 0):
                    sp.wait_ge(sem("moe_dn"), 4 * r + j - 3)
                sp.dma_start(wdn[j], A["down"][bass.ds(e, 1)].rearrange("o p k n -> (o p) k n")).then_inc(sem(f"dn_in{j}"), 16)

            each_tile(sp, load)
            for i in range(NT):
                sp.wait_ge(sem("fin_ready"), i + 1)
                sp.dma_start(out[0, i * P:(i + 1) * P], fin[i % 2]).then_inc(sem(f"out{i % 2}"), 16)
            for i in range(2):
                sp.wait_ge(sem(f"out{i}"), 16 * NT // 2)

        @block.gpsimd
        def _(pool):
            pool.memset(mhalf, -0.5).then_inc(step("mhalf_set"), 1)
            pool.wait_ge(step("mhalf_set"), nth("mhalf_set"))
            pool.dma_start(cact, A["c_col"]).then_inc(sem("c_in"), 16)
            pool.dma_start(s5_par, A["s5_par"]).then_inc(sem("s5_in"), 16)
            pool.dma_start(cst[:], A["cst"]).then_inc(sem("const_in"), 16)
            pool.dma_start(lmask[:], A["lmask"]).then_inc(sem("const_in"), 16)
            pool.dma_start(late, A["late"]).then_inc(sem("late_in"), 16)
            pool.memset(kz, 0.0).then_inc(step("kz_zero"), 1)
            pool.dma_start(nmw, A["norms"][0:1].to_broadcast([P, D])).then_inc(sem("nmw_in"), 16)
            pool.wait_ge(sem("ssq_x"), NT)
            pool.tensor_scalar(rstd, ssq, 1.0 / D, EPS, ALU.mult, ALU.add).then_inc(sem("pool_rs"), 1)
            pool.wait_ge(sem("pool_rs"), 1)
            pool.tensor_tensor(rstd, rstd, mhalf[:, 0:NT], ALU.pow).then_inc(step("rstd_x"), 1)
            pool.wait_ge(sem("mod_row"), 4)
            pool.dma_start(mod_d[0:2].rearrange("(o a) d -> o (a d)", o=1), mod_row[:, 0:2 * D]).then_inc(sem("mod_out"), 16)
            pool.wait_ge(sem("mod_out"), 16)
            pool.dma_start(b1b, mod_d[0:1].to_broadcast([P, D])).then_inc(sem("mod1_in"), 16)
            pool.dma_start(a1b, mod_d[1:2].to_broadcast([P, D])).then_inc(sem("mod1_in"), 16)
            pool.wait_ge(sem("mod1_in"), 32)
            for i in range(NT):
                pool.wait_ge(sem("h_mul"), i + 1)
                pool.tensor_tensor(x_sb[:, i], x_sb[:, i], b1b, ALU.add).then_inc(sem("h_add"), 1)
            pool.wait_ge(step("kz_full"), nth("kz_full"))
            pool.dma_start(kern_d, kz).then_inc(sem("kern_out"), 16)
            pool.wait_ge(sem("kern_out"), 16)
            for st in range(S5_L):
                pool.dma_start(s5_T[16 * st:16 * st + 16], kern_d[:, :, P - 16 * st:2 * P - 16 * st]).then_inc(sem("s5_T_in"), 16)
            pool.dma_start(ra[:, 11520:12288], A["glu"]).then_inc(sem("glu_in"), 16)
            pool.wait_ge(sem("mod_row"), 12)
            pool.dma_start(mod_d[2:6].rearrange("(o a) d -> o (a d)", o=1), mod_row[:, 2 * D:]).then_inc(sem("mod_out"), 16)
            pool.wait_ge(step("sssq"), nth("sssq"))
            pool.tensor_scalar(srstd, sssq, 1.0 / S5_W, EPS, ALU.mult, ALU.add).then_inc(sem("pool_rs"), 1)
            pool.wait_ge(sem("pool_rs"), 2)
            pool.tensor_tensor(srstd, srstd, mhalf[:, 0:NT], ALU.pow).then_inc(step("srstd"), 1)
            pool.wait_ge(sem("s5_done"), 4)
            pool.memset(ra[64:P, 0:12288], 0.0).then_inc(step("aug_zero"), 1)
            pool.wait_ge(step("aug_zero"), nth("aug_zero"))
            pool.memset(ra[64:66, 0:12288], 1.0).then_inc(sem("aug_ones"), 1)
            pool.wait_ge(sem("aug_ones"), 1)
            pool.wait_ge(sem("hb_ready"), HG_M * NT)
            pool.wait_ge(sem("win_mm"), unit_range("fq")[-1] + 1)
            chunks = lambda v: v.rearrange("p m (n t) -> p m n t", t=P)
            pool.tensor_tensor(chunks(ke), chunks(hb)[:, :, :, P - 1:P].to_broadcast([P, HG_M, NT, P]), chunks(hb), ALU.subtract).then_inc(step("d_kb"), 1)

            def distances(c):
                rnd, l = c // n_lev, c % n_lev + 1
                v = hb[:, :, 512 * rnd:512 * rnd + 512].rearrange("p m (b two x) -> p m b two x", two=2, x=LEVELS[l - 1])
                o = lev[c % 2].rearrange("p m (b two x) -> p m b two x", two=2, x=LEVELS[l - 1])
                mid = v[:, :, :, 0, LEVELS[l - 1] - 1:LEVELS[l - 1]].to_broadcast([P, HG_M, 256 // LEVELS[l - 1], LEVELS[l - 1]])
                pool.tensor_tensor(o[:, :, :, 0], mid, v[:, :, :, 0], ALU.subtract).then_inc(sem("lev_d0"), 1)
                pool.wait_ge(sem("lev_d0"), c + 1)
                pool.tensor_tensor(o[:, :, :, 1], v[:, :, :, 1], mid, ALU.subtract).then_inc(sem("lev_d"), 1)

            def keys_in(c):
                rnd, l = c // n_lev, c % n_lev + 1
                o = lev[c % 2].rearrange("p m (b two x) -> p m b two x", two=2, x=LEVELS[l - 1])[:, :, :, 0]
                v = hk[:, :, 512 * rnd:512 * rnd + 512].rearrange("p m (b two x) -> p m b two x", two=2, x=LEVELS[l - 1])[:, :, :, 0]
                pool.wait_ge(sem("lev_exp"), c + 1)
                pool.tensor_tensor(o, o, v, ALU.mult).then_inc(sem("lev_k"), 1)

            def head_powers(rnd):
                v = slice(24 * rnd, 24 * rnd + 24)
                pool.wait_ge(sem("hg_ss"), rnd + 1)
                pool.tensor_scalar(hg_r[:, v], hg_ss[:, v], 1.0 / HG_D, EPS, ALU.mult, ALU.add).then_inc(sem("pool_rs"), 1)
                pool.wait_ge(sem("pool_rs"), 3 + rnd)
                pool.tensor_tensor(hg_r[:, v], hg_r[:, v], mhalf[:, 0:24], ALU.pow).then_inc(sem("hg_r"), 1)

            pool.wait_ge(sem("win_mm"), len(UNITS))
            distances(0)
            for c in range(2 * n_lev):
                keys_in(c)
                if c + 1 < 2 * n_lev:
                    if c >= 1:
                        pool.wait_ge(sem("hg_mm"), level_done(c - 1))
                    distances(c + 1)
                if c == 0:
                    pool.wait_ge(sem("lev_k"), 1)
                    pool.wait_ge(sem("lev_d"), 2)
                    for n, v in enumerate((rc[:, 0:3072], rb[:, 6144:8192], rc[:, 6144:7168])):
                        if n == 0:
                            pool.wait_ge(sem("ke_tr"), NT)
                        if n == 1:
                            pool.wait_ge(sem("dS_mm"), NT - 1)
                        pool.memset(v, 0.0).then_inc(sem("q_zero"), 1)
                        pool.wait_ge(sem("q_zero"), n + 1)
                if c % n_lev == 0 and c:
                    head_powers(0)
            head_powers(1)

            pool.wait_ge(sem("hg_gated"), 2)
            pool.wait_ge(sem("hg_o_mm"), 2)
            pool.wait_ge(sem("cHg_ready"), NT)
            for v, src in ((gmb, mod_d[2:3]), (b2b, mod_d[3:4]), (a2b, mod_d[4:5]), (nfw, A["norms"][1:2])):
                pool.dma_start(v, src.to_broadcast([P, D])).then_inc(sem("mod2_in"), 16)
            for i in range(NT):
                pool.wait_ge(sem("fssq"), i + 1)
                pool.tensor_scalar(frstd[:, i:i + 1], fssq[:, i:i + 1], 1.0 / FOX_W, EPS, ALU.mult, ALU.add).then_inc(sem("pool_rs"), 1)
                pool.wait_ge(sem("pool_rs"), 5 + i)
                pool.tensor_tensor(frstd[:, i:i + 1], frstd[:, i:i + 1], mhalf[:, 0:1], ALU.pow).then_inc(sem("frstd"), 1)
                if i == 3:
                    pool.wait_ge(sem("mod2_in"), 64)
                    pool.tensor_tensor(a2b, a2b, nfw, ALU.mult).then_inc(step("a2_mul"), 1)
                    pool.wait_ge(step("a2_mul"), nth("a2_mul"))
                    pool.tensor_tensor(a2b, a2b, nfw, ALU.add).then_inc(step("a2_ready"), 1)

            def power(ss, r, n):
                n_pow[0] += 1
                pool.tensor_scalar(r, ss, 1.0 / n, EPS, ALU.mult, ALU.add).then_inc(sem("pool_rs"), 1)
                pool.wait_ge(sem("pool_rs"), n_pow[0])
                return pool.tensor_tensor(r, r, mhalf[:, 0:1], ALU.pow)

            n_pow = [4 + NT]
            for i in range(NT):
                pool.wait_ge(sem("ssq2"), i + 1)
                power(ssq2[:, i:i + 1], rstd2[:, i:i + 1], D).then_inc(sem("rstd2"), 1)
                pool.wait_ge(sem("h2_mul"), i + 1)
                pool.tensor_tensor(h2[i % 2], h2[i % 2], b2b, ALU.add).then_inc(sem("h2_ready"), 1)
            pool.dma_start(gfb, mod_d[5:6].to_broadcast([P, D])).then_inc(sem("last_in"), 16)
            pool.dma_start(fnw, A["norms"][2:3].to_broadcast([P, D])).then_inc(sem("last_in"), 16)
            pool.wait_ge(step("tok_set"), nth("tok_set"))
            pool.wait_ge(sem("h2_out0"), 16 * NT // 2)
            pool.wait_ge(sem("h2_out1"), 16 * NT // 2)
            pool.wait_ge(sem("mix_mm"), NT)
            for t in range(TILES):
                if t >= 4:
                    pool.wait_ge(sem("moe_T"), t - 3)
                pool.indirect_dma_start(out=rows[t % 4], out_offset=None, in_=h2_d,
                                        in_offset=bass.IndirectOffsetOnAxis(ap=tok_l[:, t:t + 1], axis=0)).then_inc(sem(f"row_in{t % 4}"), 16)
            pool.wait_ge(sem("moe_gu"), TILES)
            pool.wait_ge(sem("moe_dn"), TILES)
            for i in range(2):
                pool.wait_ge(sem(f"y_out{i}"), 16 * ((TILES + 1 - i) // 2))

            def fetch(i):
                b = i % NY
                if i >= NY:
                    pool.wait_ge(sem("x3_ready"), i - NY + 1)
                for w, v, n in ((y_a, slot_a, "a"), (y_b, slot_b, "b")):
                    pool.indirect_dma_start(out=w[b], out_offset=None, in_=y_d,
                                            in_offset=bass.IndirectOffsetOnAxis(ap=v[:, i:i + 1], axis=0)).then_inc(sem(f"y{n}_in{b}"), 16)

            pool.wait_ge(sem("slot_ready"), 2)
            for i in range(NY):
                fetch(i)
            for i in range(NT):
                pool.wait_ge(sem("ssq3"), i + 1)
                power(ssq3[:, i:i + 1], rstd3[:, i:i + 1], D).then_inc(sem("rstd3"), 1)
                if i + NY < NT:
                    fetch(i + NY)

        @block.scalar
        def _(act):
            act.wait_ge(sem("c_in"), 16)
            act.activation(cact, cact, ACT.Silu).then_inc(step("cact"), 1)
            act.wait_ge(sem("s5_in"), 16)
            act.activation(dt, dt, ACT.Exp).then_inc(step("s5_dt"), 1)
            act.wait_ge(step("s5_ph"), nth("s5_ph"))
            act.activation(p_mag, p_mag, ACT.Exp).then_inc(sem("s5_pw"), 1)
            for w in (p_re, p_im):
                act.activation(w, w, ACT.Sin, scale=TWO_PI).then_inc(sem("s5_pw"), 1)
            act.wait_ge(step("s5_rot"), nth("s5_rot"))
            for w in (s5_cos, s5_sin):
                act.activation(w, w, ACT.Sin, scale=TWO_PI).then_inc(sem("s5_cs"), 1)
            act.wait_ge(sem("x_in"), 16)
            for i in range(NT):
                act.activation(a1b, x_sb[:, i], ACT.Square, accum_out=ssq[:, i:i + 1]).then_inc(sem("ssq_x"), 1)
                act.wait_ge(sem("ssq_x"), i + 1)
            act.wait_ge(sem("kern_out"), 16)
            for i in range(NT):
                act.wait_ge(sem("h_tr"), i + 1)
                act.copy(hT[:, 0:4, i * P:(i + 1) * P],
                         bank(4 + 2 * (i % 2)).rearrange("p (k t) -> p k t", t=P)).then_inc(sem("hT_act"), 1)

            def take(name, out_of):
                for u in unit_range(name):
                    g, where = UNITS[u]
                    act.wait_ge(sem("win_mm"), u + 1)
                    for o, i, f, sc in out_of(where, bank(u % WIN_BANKS)):
                        last = act.activation(o, i, f, scale=sc)
                    last.then_inc(sem("ev_act"), 1)

            take("hq", lambda w, b: [(hq[:, w[0], 512 * w[1]:512 * w[1] + 512], b, ACT.Silu, 1.0)])
            act.wait_ge(sem("mod_out"), 32)
            take("hg", lambda i, b: [(hgate[:, i], b[:, 0:HG_W], ACT.Silu, 1.0)])
            act.wait_ge(step("s5_y_mm"), nth("s5_y_mm"))
            for b in range(4):
                m0 = 4 * (b % 2)
                act.activation(s5_y.rearrange("p s (m g c) -> p g m s c", g=2, c=S5_C)[:, b // 2, m0:m0 + 4],
                               bank(4 + b).rearrange("p (m s c) -> p m s c", m=4, s=S5_L), ACT.Gelu_apprx_tanh).then_inc(sem("s5_gelu"), 1)
            act.wait_ge(step("s5_glu_mm"), nth("s5_glu_mm"))
            act.activation(s5_gate.rearrange("p s n -> p (s n)"), bank(4, 4), ACT.Sigmoid).then_inc(step("s5_gate"), 1)
            take("fq", lambda w, b: [(qaug[0:64, 2 * w[0] + par, 512 * w[1]:512 * w[1] + 512], b[64 * par:64 * par + 64], ACT.Copy, FOX_D ** -0.5)
                                     for par in range(2)])
            act.wait_ge(sem("ev_dve"), evacuated("dve", unit_range("hf")[-1]))
            act.wait_ge(step("s5_o_tr"), nth("s5_o_tr"))
            act.activation(hk, hb, ACT.Sigmoid, scale=-1.0).then_inc(step("hk_ready"), 1)
            act.wait_ge(step("hk_ready"), nth("hk_ready"))
            for m in range(HG_M):
                if m:
                    act.wait_ge(sem("hg_lf"), m)
                for c, (f, src, sc, bias) in enumerate(((ACT.Abs, hb[:, m], 1.0, 0.0), (ACT.Exp, hg_tmp, -1.0, 0.0), (ACT.Ln, hg_tmp, 1.0, 1.0))):
                    last = act.activation(hg_tmp, src, f, scale=sc, bias=bias)
                    last.then_inc(sem("hg_ln" if c == 2 else "hg_abs"), 1)
                    if c < 2:
                        act.wait_ge(sem("hg_abs"), 2 * m + c + 1)

            act.wait_ge(sem("flog"), 1)
            for c, (f, src, sc, bias) in enumerate(((ACT.Abs, flog, 1.0, 0.0), (ACT.Exp, fln, -1.0, 0.0), (ACT.Ln, fln, 1.0, 1.0))):
                act.activation(fln, src, f, scale=sc, bias=bias).then_inc(sem("fln"), 1)
                act.wait_ge(sem("fln"), c + 1)
            act.wait_ge(sem("hb_ready"), HG_M * NT)
            act.wait_ge(step("d_kb"), nth("d_kb"))
            act.activation(ke, ke, ACT.Exp).then_inc(step("e_kb"), 1)
            act.activation(efin.rearrange("p (m n) -> p m n", m=HG_M), hb[:, :, P - 1::P], ACT.Exp).then_inc(step("efin"), 1)
            act.wait_ge(sem("win_mm"), len(UNITS))
            act.activation(qe, hb, ACT.Exp).then_inc(step("e_b"), 1)
            for c in range(2 * n_lev):
                act.wait_ge(sem("lev_d"), c + 1)
                act.activation(lev[c % 2], lev[c % 2], ACT.Exp).then_inc(sem("lev_exp"), 1)

            def fox_take(i):
                act.wait_ge(sem("fo_tr"), i + 1)
                act.copy(cFox[:, :, i * P:(i + 1) * P], bank(6 + i % 2)[:, 0:FOX_W].rearrange("p (m t) -> p m t", m=3)).then_inc(sem("cFox_ready"), 1)

            act.wait_ge(sem("cHg_ready"), NT)
            for u, (i, h) in enumerate(units):
                act.wait_ge(sem("f_max"), u + 1)
                if u >= 2:
                    act.wait_ge(sem("f_T"), u - 1)
                w = (i + 1) * P
                act.activation(prob[u % 2][:, 0:w], psum[:, 1024 * (u % 2):1024 * (u % 2) + w], ACT.Exp, bias=negmax[:, u:u + 1],
                               accum_out=rowsum[:, u:u + 1]).then_inc(sem("f_exp"), 1)
                if i >= 4:
                    act.wait_ge(sem("f_T"), u + 1)
                    if u >= 2:
                        act.wait_ge(sem("f_pv"), u - 1)
                    act.copy(probT[u % 2][:, 4:i + 1], bank(5)[:, 0:(i - 3) * P].rearrange("p (k q) -> p k q", q=P)).then_inc(sem("fT_act"), 1)
                if i == 3 or (i == 4 and h < 2):
                    k = u - 3 * FOX_H
                    if k == 0:
                        act.wait_ge(sem("w_out_in"), 16)
                        act.wait_ge(sem("late_in"), 16)
                    last = act.activation(w_out[:, k], w_out[:, k], ACT.Copy, scale=wrow[:, k:k + 1])
                    if k == KD - 1:
                        last.then_inc(step("w_scaled"), 1)
                if i >= 1 and h == 5:
                    fox_take(i - 1)
            fox_take(NT - 1)

            act.wait_ge(sem("f_pv"), len(units))
            for i in range(NT):
                if i >= 1:
                    act.wait_ge(sem("ssq2"), i)
                act.wait_ge(sem("x2_ready"), i + 1)
                act.activation(sq2, x2[:, i], ACT.Square, accum_out=ssq2[:, i:i + 1]).then_inc(sem("ssq2"), 1)
                act.wait_ge(sem("h2_tr"), i + 1)
                if i >= 2:
                    act.wait_ge(sem("route_mm"), i - 1)
                act.copy(h2T[i % 2][:, 0:4], bank(4).rearrange("p (k t) -> p k t", t=P)).then_inc(sem("h2T_act"), 1)
            act.wait_ge(step("rt_sub"), nth("rt_sub"))
            act.activation(rt[1], rt[0], ACT.Exp).then_inc(step("rt_exp"), 1)

            def take_rows(t, j):
                act.wait_ge(sem("moe_T"), t + 1)
                if not (isinstance(t, int) and t < 2):
                    act.wait_ge(sem("moe_gu"), t - 1)
                act.copy(rowT[j % 2][:, 0:4], bank(2).rearrange("p (k t) -> p k t", t=P)).then_inc(sem("rowT_act"), 1)

            def take_answer(t, j, r):
                act.wait_ge(sem("y_taken"), t + 1)
                act.dma_start(y_d[bass.ds(t * P, P)], answer[j % 2]).then_inc(sem(f"y_out{j % 2}"), 16)

            def gate(t, j, r):
                act.wait_ge(sem("moe_gu"), t + 1)
                if not (isinstance(t, int) and t < 2):
                    act.wait_ge(sem("hid_ready"), t - 1)
                act.activation(silu[j % 2], bank(j % 2)[:, 0:FF], ACT.Silu).then_inc(sem("silu_ready"), 1)
                if not (isinstance(t, int) and t == TILES - 1):
                    take_rows(t + 1, (j + 1) % 4)
                if not (isinstance(t, int) and t == 0):
                    take_answer(t - 1, (j - 1) % 4, r if j else r - 1)

            take_rows(0, 0)
            each_tile(act, gate)
            take_answer(TILES - 1, (TILES - 1) % 4, TILES // 4)

            for i in range(NT):
                act.wait_ge(sem("x3_ready"), i + 1)
                if i >= 1:
                    act.wait_ge(sem("ssq3"), i)
                act.activation(sq3, x2[:, i], ACT.Square, accum_out=ssq3[:, i:i + 1]).then_inc(sem("ssq3"), 1)

        @block.vector
        def _(dve):
            n_own = [0]

            def link(ins):
                n_own[0] += 1
                ins.then_inc(sem("dve_own"), 1)
                dve.wait_ge(sem("dve_own"), n_own[0])

            def mod_rows(a, b):
                for n in range(a, b):
                    row = mod_row[:, n * ADA_N:(n + 1) * ADA_N]
                    dve.wait_ge(sem("ada_mm"), n + 1)
                    dve.tensor_tensor(row, bank(n % 4)[0:1], row, ALU.add).then_inc(sem("mod_row"), 1)

            dve.wait_ge(sem("const_in"), 32)
            dve.wait_ge(step("s5_dt"), nth("s5_dt"))
            link(dve.tensor_tensor(lr, are, dt, ALU.mult))
            link(dve.tensor_tensor(th, aim, dt, ALU.mult))
            link(dve.tensor_scalar(th, th, 1.0 / (2 * np.pi), None, ALU.mult))

            def whole_turns_off(x, scratch):
                link(dve.tensor_scalar(scratch, x, ROUND, ROUND, ALU.add, ALU.subtract))
                return dve.tensor_tensor(x, x, scratch, ALU.subtract)

            link(whole_turns_off(th, u0))
            n17 = cst[:, C_POW:C_POW + 17].unsqueeze(1).to_broadcast([P, S5_M, 17])
            link(dve.tensor_tensor(p_mag, b3(lr, 17), n17, ALU.mult))
            link(dve.tensor_tensor(p_im, b3(th, 17), n17, ALU.mult))
            link(dve.tensor_scalar(p_re, p_im, 0.25, None, ALU.add))
            link(whole_turns_off(p_im, p_tmp))
            whole_turns_off(p_re, p_tmp).then_inc(step("s5_ph"), 1)
            link(dve.tensor_scalar(ph8, th, float(S5_L), None, ALU.mult))
            link(whole_turns_off(ph8, u0))
            jrow = cst[:, C_J:C_J + P].unsqueeze(1).to_broadcast([P, S5_M, S5_J])
            link(dve.tensor_tensor(s5_sin.rearrange("p (m j) -> p m j", m=S5_M), b3(ph8, S5_J), jrow, ALU.mult))
            link(dve.tensor_scalar(s5_cos, s5_sin, 0.25, None, ALU.add))
            link(whole_turns_off(s5_sin, s5_tab[0]))
            whole_turns_off(s5_cos, s5_tab[0]).then_inc(step("s5_rot"), 1)
            dve.wait_ge(sem("s5_pw"), 3)
            link(dve.tensor_tensor(p_re, p_re, p_mag, ALU.mult))
            link(dve.tensor_tensor(p_im, p_im, p_mag, ALU.mult))
            link(dve.tensor_scalar(am1, p_re[:, :, 1], -1.0, None, ALU.add))
            link(dve.tensor_tensor(u0, are, are, ALU.mult))
            link(dve.tensor_tensor(u1, aim, aim, ALU.mult))
            link(dve.tensor_tensor(den, u0, u1, ALU.add))
            link(dve.reciprocal(den, den))
            link(dve.tensor_tensor(u0, am1, are, ALU.mult))
            link(dve.tensor_tensor(u1, p_im[:, :, 1], aim, ALU.mult))
            link(dve.tensor_tensor(u0, u0, u1, ALU.add))
            link(dve.tensor_tensor(wr, u0, den, ALU.mult))
            link(dve.tensor_tensor(u0, p_im[:, :, 1], are, ALU.mult))
            link(dve.tensor_tensor(u1, am1, aim, ALU.mult))
            link(dve.tensor_tensor(u0, u0, u1, ALU.subtract))
            link(dve.tensor_tensor(wi, u0, den, ALU.mult))

            def complex_mul(out_re, out_im, ar, ai, br, bi, shape, minus_im=False):
                n = int(np.prod(shape))
                names = "xyz"[:len(shape)]
                t, v = [w[:, 0:n].rearrange(f"p ({' '.join(names)}) -> p {' '.join(names)}",
                                            **{k: q for k, q in zip(names[1:], shape[1:])}) for w in s5_tab]
                dve.tensor_tensor(t, ar, br, ALU.mult)
                link(dve.tensor_tensor(v, ai, bi, ALU.mult))
                link(dve.tensor_tensor(out_re, t, v, ALU.subtract))
                dve.tensor_tensor(t, ar, bi, ALU.mult)
                link(dve.tensor_tensor(v, ai, br, ALU.mult))
                if minus_im:
                    return dve.scalar_tensor_tensor(out=out_im, in0=t, scalar=-1.0, in1=v, op0=ALU.mult, op1=ALU.subtract)
                return dve.tensor_tensor(out_im, t, v, ALU.add)

            dve.wait_ge(sem("ada_b_in"), 16)
            mod_rows(0, 4)
            link(complex_mul(s5_bb[:, 0], s5_bb[:, 1], b3(wr, S5_C), b3(wi, S5_C), s5_B[:, 0], s5_B[:, 1], (S5_M, S5_C)))
            full = [P, S5_M, S5_L, S5_C]
            complex_mul(s5_BA[:, 0], s5_BA[:, 1],
                        p_re[:, :, 9:17].unsqueeze(3).to_broadcast(full), p_im[:, :, 9:17].unsqueeze(3).to_broadcast(full),
                        s5_bb[:, 0].unsqueeze(2).to_broadcast(full), s5_bb[:, 1].unsqueeze(2).to_broadcast(full),
                        full[1:]).then_inc(step("s5_BA"), 1)
            dve.wait_ge(step("s5_BA"), nth("s5_BA"))
            for mh in range(2):
                ms = slice(4 * mh, 4 * mh + 4)
                nine = [P, 4, 9, S5_C]
                last = complex_mul(s5_CA[:, 0, ms], s5_CA[:, 1, ms],
                                   p_re[:, ms, 0:9].unsqueeze(3).to_broadcast(nine), p_im[:, ms, 0:9].unsqueeze(3).to_broadcast(nine),
                                   s5_Ct[:, 0, ms].unsqueeze(2).to_broadcast(nine), s5_Ct[:, 1, ms].unsqueeze(2).to_broadcast(nine),
                                   nine[1:], minus_im=True)
                link(last)
            dve.tensor_copy(s5_R.rearrange("p (m j) -> p m j", m=S5_M), b3(p_mag[:, :, 8], S5_J)).then_inc(step("s5_CA"), 1)
            dve.wait_ge(step("s5_CA"), nth("s5_CA"))
            link(dve.memset(s5_R.rearrange("p (m j) -> p m j", m=S5_M)[:, :, 0:1], 0.0))

            dve.wait_ge(sem("mod1_in"), 32)
            dve.wait_ge(sem("nmw_in"), 16)
            link(dve.scalar_tensor_tensor(out=a1b, in0=a1b, scalar=1.0, in1=nmw, op0=ALU.add, op1=ALU.mult))
            dve.wait_ge(step("rstd_x"), nth("rstd_x"))
            for i in range(NT):
                dve.scalar_tensor_tensor(out=x_sb[:, i], in0=x_sb[:, i], scalar=rstd[:, i:i + 1], in1=a1b,
                                         op0=ALU.mult, op1=ALU.mult).then_inc(sem("h_mul"), 1)
            dve.wait_ge(step("s5_W_tr"), nth("s5_W_tr"))
            for b in range(4):
                dve.tensor_copy(s5_W.rearrange("p m a x -> p (m a x)")[:, 512 * b:512 * b + 512], bank(4 + b)).then_inc(sem("s5_W"), 1)
            mod_rows(4, 6)
            dve.wait_ge(step("s5_kern"), nth("s5_kern"))
            dve.wait_ge(step("kz_zero"), nth("kz_zero"))
            for par in range(2):
                link(dve.tensor_copy(kz.rearrange("c (m g) x -> c g m x", g=2)[:, par, :, P:2 * P],
                                     bank(4 + 2 * par, 2)[0:S5_C].rearrange("c (m x) -> c m x", m=S5_M)))
            dd = s5_tab[0][0:S5_C, 0:S5_G * S5_C].rearrange("c (g x) -> c g x", g=S5_G)
            link(dve.tensor_tensor(dd, b3(s5_D, S5_C), cst[0:S5_C, 0:S5_C].unsqueeze(1).to_broadcast([S5_C, S5_G, S5_C]), ALU.mult))
            dve.tensor_tensor(kz[:, :, P:P + S5_C], kz[:, :, P:P + S5_C], dd, ALU.add).then_inc(step("kz_full"), 1)
            mod_rows(6, 12)
            dve.wait_ge(sem("kern_out"), 16)
            for i in range(NT):
                dve.wait_ge(sem("h_tr"), i + 1)
                dve.tensor_copy(hT[:, 4:8, i * P:(i + 1) * P],
                                bank(5 + 2 * (i % 2)).rearrange("p (k t) -> p k t", t=P)).then_inc(sem("hT_dve"), 1)

            def take(name, out_of):
                for u in unit_range(name):
                    g, where = UNITS[u]
                    dve.wait_ge(sem("win_mm"), u + 1)
                    for o, i in out_of(where, bank(u % WIN_BANKS)):
                        last = dve.tensor_copy(o, i)
                    last.then_inc(sem("ev_dve"), 1)

            take("su", lambda st, b: [(s5_Z[:, :, st], b[:, 0:S5_W].rearrange("p (g c) -> p g c", g=S5_G))])
            dve.wait_ge(step("s5_U_tr"), nth("s5_U_tr"))
            for b in range(4):
                dve.tensor_copy(s5_U.rearrange("p g j -> p (g j)")[:, 512 * b:512 * b + 512], bank(4 + b)).then_inc(sem("s5_U"), 1)
            dve.wait_ge(sem("mod_out"), 32)
            take("hi", lambda i, b: [(hv[:, i], b[:, 0:HG_W])])
            dve.wait_ge(step("s5_V_mm"), nth("s5_V_mm"))
            dve.wait_ge(sem("s5_cs"), 2)
            v_re, v_im = bank(4, 2), bank(6, 2)
            t, v = s5_t
            dve.tensor_tensor(t, v_re, s5_cos, ALU.mult)
            link(dve.tensor_tensor(v, v_im, s5_sin, ALU.mult))
            link(dve.tensor_tensor(s5_V[:, 0], t, v, ALU.add))
            dve.tensor_tensor(t, v_im, s5_cos, ALU.mult)
            link(dve.tensor_tensor(v, v_re, s5_sin, ALU.mult))
            link(dve.tensor_tensor(s5_V[:, 1], t, v, ALU.subtract))
            for a in range(2):
                link(dve.tensor_tensor_scan(out=s5_V[:, a], data0=s5_R, data1=s5_V[:, a], initial=0.0, op0=ALU.mult, op1=ALU.add))
            xr, xi = s5_V[:, 0], s5_V[:, 1]
            mj = lambda w: w.rearrange("p (m j) -> p m j", m=S5_M)
            for a, (op, x0, x1) in enumerate(((ALU.subtract, xr, xi), (ALU.add, xi, xr))):
                dve.tensor_tensor(t, x0, s5_cos, ALU.mult)
                link(dve.tensor_tensor(v, x1, s5_sin, ALU.mult))
                dve.memset(s5_X[a][:, :, 0:1], 0.0).then_inc(sem("s5_X0"), 1)
                dve.wait_ge(sem("s5_X0"), a + 1)
                dve.tensor_tensor(s5_X[a][:, :, 1:S5_J], mj(t)[:, :, 0:S5_J - 1], mj(v)[:, :, 0:S5_J - 1], op).then_inc(sem("s5_X"), 1)
                dve.wait_ge(sem("s5_X"), a + 1)
            take("hf", lambda w, b: [(hb[:, w[0], 512 * w[1]:512 * w[1] + 512], b)])
            dve.wait_ge(step("s5_y_tr"), nth("s5_y_tr"))
            for b in range(4):
                dve.tensor_copy(s5_yT.rearrange("p c s j -> p (c s j)")[:, 512 * b:512 * b + 512], bank(4 + b)).then_inc(sem("s5_yT"), 1)
            take("fv", lambda i, b: [(fv[:, i], b[:, 0:VW])])
            dve.wait_ge(sem("late_in"), 16)
            dve.wait_ge(sem("ev_dve"), evacuated("dve", unit_range("fv")[-1]))
            f3 = flog.rearrange("p (i h) -> p i h", h=FOX_H)
            dve.tensor_tensor(f3, fv[:, :, FOX_W:VW], fbias.unsqueeze(1).to_broadcast([P, NT, FOX_H]), ALU.add).then_inc(sem("flog"), 1)
            dve.wait_ge(step("s5_gate"), nth("s5_gate"))
            link(dve.tensor_tensor(s5_y, s5_y, s5_gate, ALU.mult))
            link(dve.tensor_tensor(s5_sq, s5_y, s5_y, ALU.mult))
            dve.tensor_reduce(sssq, s5_sq, AX_X, ALU.add).then_inc(step("sssq"), 1)
            dve.wait_ge(step("srstd"), nth("srstd"))
            dve.tensor_tensor(s5_y, s5_y, b3(srstd, S5_W), ALU.mult).then_inc(step("s5_o"), 1)
            dve.wait_ge(step("s5_o_tr"), nth("s5_o_tr"))
            for b in range(4):
                c, s0 = b // 2, 4 * (b % 2)
                dve.tensor_copy(cS5[:, c].rearrange("p (j s) -> p s j", s=S5_L)[:, s0:s0 + 4],
                                bank(4 + b).rearrange("p (s j) -> p s j", s=4)).then_inc(sem("s5_done"), 1)
            for m in range(HG_M):
                dve.wait_ge(sem("hg_ln"), m + 1)
                dve.scalar_tensor_tensor(out=hb[:, m], in0=hb[:, m], scalar=0.0, in1=hg_tmp, op0=ALU.min, op1=ALU.subtract).then_inc(sem("hg_lf"), 1)
                dve.wait_ge(sem("hg_lf"), m + 1)
                for n in range(NT):
                    dve.tensor_tensor_scan(out=hb[:, m, n * P:(n + 1) * P], data0=ones, data1=hb[:, m, n * P:(n + 1) * P], initial=0.0,
                                           op0=ALU.mult, op1=ALU.add).then_inc(sem("hb_ready"), 1)
            take("fk", lambda w, b: [(kaug[0:64, 2 * w[0] + par, 512 * w[1]:512 * w[1] + 512], b[64 * par:64 * par + 64]) for par in range(2)])

            def take_scores(rnd, l, a=0, b=HG_H):
                for h in range(a, b):
                    c = (rnd * (1 + n_lev) + l) * HG_H + h
                    if l:
                        dve.wait_ge(sem("hg_taken"), c - HG_H + 1 if l > 1 else c - h - HG_H + 2 * (h // 2) + 2)
                    dve.wait_ge(sem("hg_mm"), c + 1)
                    four_ = bank(c % 4).rearrange("p (n t) -> p n t", n=4)
                    if l == 0:
                        dve.tensor_tensor(sT[:, h], four_, ident.unsqueeze(1).to_broadcast([P, 4, P]), ALU.mult).then_inc(sem("hg_taken"), 1)
                    else:
                        m, n0 = h // 2, 2 * (h % 2)
                        dve.copy_predicated(sT[:, 2 * m:2 * m + 2, n0:n0 + 2].rearrange("p g n t -> p n g t"),
                                            masks[:, l].unsqueeze(1).unsqueeze(1).to_broadcast([P, 2, 2, P]),
                                            four_.rearrange("p (n g) t -> p n g t", n=2)).then_inc(sem("hg_taken"), 1)

            def halves(v, l):
                return v.rearrange("p m (b two x) -> p m b two x", two=2, x=LEVELS[l - 1])

            dve.wait_ge(sem("fln"), 3)
            dve.scalar_tensor_tensor(out=flog, in0=flog, scalar=0.0, in1=fln, op0=ALU.min, op1=ALU.subtract).then_inc(sem("flog"), 1)
            dve.tensor_copy(ident16[:], ident).then_inc(sem("mask16"), 1)
            dve.tensor_copy(neg16[:], cst[:, C_NEG:C_NEG + P]).then_inc(sem("mask16"), 1)
            dve.wait_ge(step("e_kb"), nth("e_kb"))
            dve.tensor_tensor(ke, ke, hk, ALU.mult).then_inc(step("ke_ready"), 1)
            for rnd in range(2):
                rs = slice(512 * rnd, 512 * rnd + 512)
                if rnd:
                    dve.wait_ge(sem("hg_gated"), rnd)
                take_scores(rnd, 0)
                if rnd == 0:
                    dve.wait_ge(step("f_tr"), nth("f_tr"))
                    dve.wait_ge(sem("aug_ones"), 1)
                    link(dve.tensor_tensor_scan(out=cum, data0=cst[0:FOX_H, C_ONE:C_ONE + 1].to_broadcast([FOX_H, T]), data1=bank(4, 2)[0:FOX_H],
                                                initial=0.0, op0=ALU.mult, op1=ALU.add))
                    dve.tensor_scalar(ncum, cum, -1.0, None, ALU.mult).then_inc(step("cum_ready"), 1)
                    for n in range(NT):
                        dve.wait_ge(sem("ke_tr"), n + 1)
                        dve.tensor_copy(keT[n], bank(4 + n % 4)[:, 0:HG_W]).then_inc(sem("keT_ready"), 1)
                    for c in range(NT - 1):
                        dve.wait_ge(sem("dS_mm"), min(c // 2 * 2 + 2, NT - 1))
                        o = 2048 + 512 * (c // 2) + 192 * (c % 2)
                        dS = psum[:, o:o + 192]
                        if c == 0:
                            dve.tensor_copy(hg_S[:, 0], dS).then_inc(sem("hg_S"), 1)
                        else:
                            dve.wait_ge(sem("hg_S"), c)
                            dve.wait_ge(step("efin"), nth("efin"))
                            link(dve.tensor_tensor(hg_S[:, c].rearrange("p (m v) -> p m v", m=HG_M), hg_S[:, c - 1].rearrange("p (m v) -> p m v", m=HG_M),
                                                   b3(efin.rearrange("p (m n) -> p m n", m=HG_M)[:, :, c], HG_D), ALU.mult))
                            dve.tensor_tensor(hg_S[:, c], hg_S[:, c], dS, ALU.add).then_inc(sem("hg_S"), 1)
                    dve.wait_ge(sem("q_zero"), 3)
                for l in range(1, 1 + n_lev):
                    c = rnd * n_lev + l - 1
                    if l > 1:
                        take_scores(rnd, l - 1, 0, 4)
                    dve.wait_ge(sem("lev_exp"), c + 1)
                    if c >= 2:
                        dve.wait_ge(sem("hg_mm"), level_done(c - 2))
                    for par in range(2):
                        h = slice(64 * par, 64 * par + 64)
                        whole = lambda v: halves(v, l)[h, :, :, 1]
                        if c % 2 == 0:
                            q3 = rc[:, 0:3072].rearrange("p (m g t) -> p m g t", m=HG_M, g=2)[:, :, par]
                            last = dve.tensor_tensor(whole(q3), whole(lev[0]), whole(hq[:, :, rs]), ALU.mult)
                        else:
                            q2 = rb[:, 6144:8192].rearrange("p (m g t) -> p m g t", m=2, g=2)[:, :, par]
                            dve.tensor_tensor(whole(q2), whole(lev[1][:, 0:2]), whole(hq[:, 0:2, rs]), ALU.mult)
                            q1 = rc[:, 6144:7168].rearrange("p (m g t) -> p m g t", m=1, g=2)[:, :, par]
                            last = dve.tensor_tensor(whole(q1), whole(lev[1][:, 2:3]), whole(hq[:, 2:3, rs]), ALU.mult)
                    last.then_inc(sem("lev_q"), 1)
                    if rnd == 0 and l == 1:
                        dve.wait_ge(step("e_b"), nth("e_b"))
                        dve.tensor_tensor(qe, qe, hq, ALU.mult).then_inc(step("qe_ready"), 1)
                    if l > 1:
                        take_scores(rnd, l - 1, 4)
                take_scores(rnd, n_lev)
                dve.wait_ge(sem("hg_o_mm"), rnd + 1)
                for b in range(4):
                    par, n0 = b // 2, 2 * (b % 2)
                    dve.tensor_copy(hg_o.rearrange("p (n m g) v -> p n m g v", m=HG_M, g=2)[:, n0:n0 + 2, :, par],
                                    bank(4 + b)[:, 0:384].rearrange("p (n m v) -> p n m v", n=2, m=HG_M)).then_inc(sem("hg_o_taken"), 1)
                dve.wait_ge(sem("hg_o_taken"), 4 * rnd + 4)
                link(dve.tensor_tensor(hg_sq, hg_o, hg_o, ALU.mult))
                dve.tensor_reduce(hg_ss[:, 24 * rnd:24 * rnd + 24], hg_sq, AX_X, ALU.add).then_inc(sem("hg_ss"), 1)
                dve.wait_ge(sem("hg_r"), rnd + 1)
                link(dve.tensor_tensor(hg_o, hg_o, b3(hg_r[:, 24 * rnd:24 * rnd + 24], HG_D), ALU.mult))
                g = hgate[:, 4 * rnd:4 * rnd + 4].rearrange("p n w -> p (n w)")
                dve.tensor_tensor(g, hg_o.rearrange("p a v -> p (a v)"), g, ALU.mult).then_inc(sem("hg_gated"), 1)
            for n in range(NT):
                dve.wait_ge(sem("hg_o_tr"), n + 1)
                dve.tensor_copy(cHg[:, :, n * P:(n + 1) * P], bank(4 + n % 4)[:, 0:HG_W].rearrange("p (m t) -> p m t", m=HG_M)).then_inc(sem("cHg_ready"), 1)

            def maxima(u):
                i, h = units[u]
                dve.wait_ge(sem("f_qk"), u + 1)
                dve.tensor_reduce(negmax[:, u:u + 1], psum[:, 1024 * (u % 2):1024 * (u % 2) + (i + 1) * P], AX_X, ALU.max, negate=True).then_inc(sem("f_max"), 1)

            def fox_norm(i):
                dve.wait_ge(sem("f_pv"), FOX_H * (i + 1))
                dve.wait_ge(sem("f_exp"), FOX_H * (i + 1))
                hs = slice(FOX_H * i, FOX_H * (i + 1))
                link(dve.reciprocal(rinv[:, hs], rowsum[:, hs]))
                o = fo[i % 2]
                if i >= 2:
                    dve.wait_ge(sem("fo_tr"), i - 1)
                link(dve.tensor_tensor(o.rearrange("p (h d) -> p h d", h=FOX_H), bank(6 + i % 2)[:, 0:FOX_W].rearrange("p (h d) -> p h d", h=FOX_H),
                                       b3(rinv[:, hs], FOX_D), ALU.mult))
                link(dve.tensor_tensor(fsq, o, o, ALU.mult))
                dve.tensor_reduce(fssq[:, i:i + 1], fsq, AX_X, ALU.add).then_inc(sem("fssq"), 1)

            def fox_scale(i):
                dve.wait_ge(sem("frstd"), i + 1)
                dve.tensor_scalar(fo[i % 2], fo[i % 2], frstd[:, i:i + 1], None, ALU.mult).then_inc(sem("fo_ready"), 1)

            maxima(0)
            for u in range(len(units)):
                i, h = units[u]
                if u + 1 < len(units):
                    maxima(u + 1)
                dve.wait_ge(sem("f_T"), u + 1)
                if u >= 2:
                    dve.wait_ge(sem("f_pv"), u - 1)
                w = min(4, i + 1)
                dve.tensor_copy(probT[u % 2][:, 0:w], bank(4)[:, 0:w * P].rearrange("p (k q) -> p k q", q=P)).then_inc(sem("fT_dve"), 1)
                if i >= 1 and h == 1:
                    fox_norm(i - 1)
                if i >= 1 and h == 2:
                    fox_scale(i - 1)
            fox_norm(NT - 1)
            fox_scale(NT - 1)

            dve.wait_ge(sem("x2_in"), 16)
            dve.wait_ge(sem("mod2_in"), 64)
            dve.wait_ge(sem("f_pv"), len(units))

            def add_mix(i):
                dve.wait_ge(sem("mix_mm"), i + 1)
                if i >= 2:
                    dve.wait_ge(sem("x2_ready"), i - 1)
                dve.tensor_tensor(mix_t[i % 2], bank(2 * (i % 2), 2), gmb, ALU.mult).then_inc(sem("mix_taken"), 1)
                dve.wait_ge(sem("mix_taken"), i + 1)
                dve.tensor_tensor(x2[:, i], x2[:, i], mix_t[i % 2], ALU.add).then_inc(sem("x2_ready"), 1)

            add_mix(0)
            for i in range(NT):
                dve.wait_ge(sem("rstd2"), i + 1)
                dve.wait_ge(step("a2_ready"), nth("a2_ready"))
                if i >= 2:
                    dve.wait_ge(sem(f"h2_out{i % 2}"), 16 * (i // 2))
                    dve.wait_ge(sem("h2_tr"), i - 1)
                dve.scalar_tensor_tensor(out=h2[i % 2], in0=x2[:, i], scalar=rstd2[:, i:i + 1], in1=a2b, op0=ALU.mult, op1=ALU.mult).then_inc(sem("h2_mul"), 1)
                if i + 1 < NT:
                    add_mix(i + 1)
                dve.wait_ge(sem("h2_tr"), i + 1)
                if i >= 2:
                    dve.wait_ge(sem("route_mm"), i - 1)
                dve.tensor_copy(h2T[i % 2][:, 4:8], bank(5).rearrange("p (k t) -> p k t", t=P)).then_inc(sem("h2T_dve"), 1)

            three = lambda v: v.rearrange("p (i e) -> p i e", e=NE)
            L, pr, score, rank, sel, mask, pm, comb, sl, hit, tmp, tmp2 = rt
            st, mx, gs, gr, tot_, cnt, nt_, end_, base_, s1, s2, s3 = rs_
            dve.wait_ge(sem("route_mm"), NT)
            link(dve.tensor_copy(L, bank(6)[:, 0:P]))
            link(dve.tensor_reduce(mx[:, 0:NT], three(L), AX_X, ALU.max))
            dve.tensor_tensor(three(L), three(L), b3(mx[:, 0:NT], NE), ALU.subtract).then_inc(step("rt_sub"), 1)
            dve.wait_ge(step("rt_exp"), nth("rt_exp"))
            link(dve.tensor_reduce(st[:, 0:NT], three(pr), AX_X, ALU.add))
            link(dve.reciprocal(st[:, 0:NT], st[:, 0:NT]))
            link(dve.tensor_tensor(three(pr), three(pr), b3(st[:, 0:NT], NE), ALU.mult))

            def ranks(v, r, g):
                n = v.shape[1]
                link(dve.tensor_copy(r, cst[:, C_RANK:C_RANK + 4].unsqueeze(1).to_broadcast([P, n, 4])))
                for d in range(1, 4):
                    w = g[:, :, 0:4 - d]
                    link(dve.tensor_tensor(w, v[:, :, 0:4 - d], v[:, :, d:4], ALU.is_ge))
                    link(dve.tensor_tensor(r[:, :, d:4], r[:, :, d:4], w, ALU.add))
                    link(dve.tensor_tensor(r[:, :, 0:4 - d], r[:, :, 0:4 - d], w, ALU.subtract))

            four = lambda v: v.rearrange("p (n x) -> p n x", x=PG)
            ranks(four(pr), four(rank), four(tmp))
            link(dve.tensor_scalar(sel, rank, 2.0, None, ALU.is_lt))
            link(dve.tensor_tensor(tmp, pr, sel, ALU.mult))
            link(dve.tensor_reduce(gs, four(tmp), AX_X, ALU.add))
            ranks(four(gs), four(gr), four(s1))
            link(dve.tensor_scalar(gr, gr, 1.0, None, ALU.is_lt))
            dve.tensor_tensor(four(mask), four(sel), b3(gr, PG), ALU.mult).then_inc(step("chosen"), 1)
            dve.wait_ge(step("chosen"), nth("chosen"))
            link(dve.tensor_tensor(pm, pr, mask, ALU.mult))
            link(dve.tensor_reduce(st[:, 0:NT], three(pm), AX_X, ALU.add))
            link(dve.reciprocal(st[:, 0:NT], st[:, 0:NT]))
            link(dve.tensor_tensor(three(comb), three(pm), b3(st[:, 0:NT], NE), ALU.mult))
            dve.wait_ge(step("count_mm"), nth("count_mm"))
            before, total = three(bank(7)[:, 0:P]), three(bank(7)[:, P:2 * P])
            link(dve.memset(three(tmp)[:, 0], 0.0))
            for i in range(1, NT):
                link(dve.tensor_tensor(three(tmp)[:, i], three(tmp)[:, i - 1], total[:, i - 1], ALU.add))
            cnt = cnt[:, 0:NE]
            link(dve.tensor_tensor(cnt, three(tmp)[:, NT - 1], total[:, NT - 1], ALU.add))
            link(dve.tensor_tensor(three(sl), before, three(tmp), ALU.add))
            link(dve.tensor_tensor(thr, b3(cnt, NT), cst[:, C_THR:C_THR + 8].unsqueeze(1).to_broadcast([P, NE, NT]), ALU.is_gt))
            nt_, end_, base_ = nt_[:, 0:NE], end_[:, 0:NE], base_[:, 0:NE]
            link(dve.tensor_reduce(nt_, thr, AX_X, ALU.add))
            link(dve.tensor_tensor_scan(out=end_, data0=ones[:, 0:NE], data1=nt_, initial=0.0, op0=ALU.mult, op1=ALU.add))
            link(dve.tensor_tensor(til, b3(cst[:, C_J:C_J + 32], NE), end_.unsqueeze(1).to_broadcast([P, 32, NE]), ALU.is_ge))
            link(dve.tensor_reduce(s3, til, AX_X, ALU.add))
            link(dve.tensor_scalar(s3, s3, float(NE - 1), None, ALU.min))
            dve.tensor_copy(expert_i, s3).then_inc(step("expert_ready"), 1)
            link(dve.tensor_tensor(base_, end_, nt_, ALU.subtract))
            link(dve.tensor_scalar(base_, base_, float(P), 1.0, ALU.mult, ALU.add))
            link(dve.tensor_tensor(three(sl), three(sl), base_.unsqueeze(1).to_broadcast([P, NT, NE]), ALU.add))
            link(dve.tensor_tensor(sl, sl, mask, ALU.mult))
            both, slots = s1[:, 0:2 * NT], rs_[10][:, 0:2 * NT]
            s1, s2 = both[:, 0:NT], both[:, NT:]
            link(dve.tensor_reduce(s2, three(sl), AX_X, ALU.max))
            link(dve.tensor_reduce(s1, three(sl), AX_X, ALU.add))
            link(dve.tensor_tensor(s1, s1, s2, ALU.subtract))
            link(dve.tensor_scalar(slots, both, -1.0, None, ALU.add))
            whole, rest = gs[:, 0:2 * NT], gr[:, 0:2 * NT]
            link(dve.tensor_scalar(whole, slots, 1.0 / P, 0.5 / P - 0.5, ALU.mult, ALU.add))
            link(dve.tensor_scalar(whole, whole, ROUND, ROUND, ALU.add, ALU.subtract))
            link(dve.scalar_tensor_tensor(out=rest, in0=whole, scalar=-float(P), in1=slots, op0=ALU.mult, op1=ALU.add))
            link(dve.tensor_tensor(number, b3(whole, 32), cst[:, C_J:C_J + 32].unsqueeze(1).to_broadcast([P, 2 * NT, 32]), ALU.is_equal))
            for v in (number[:, 0:NT], number[:, NT:]):
                dve.tensor_tensor(v, v, b3(cst[:, C_TOK:C_TOK + NT], 32), ALU.mult).then_inc(sem("numbered"), 1)
            dve.tensor_tensor(place, b3(rest, P), cst[:, C_J:C_J + P].unsqueeze(1).to_broadcast([P, 2 * NT, P]), ALU.is_equal).then_inc(step("picks"), 1)
            dve.wait_ge(step("list_mm"), nth("list_mm"))
            dve.tensor_copy(tok_l, bank(7)[:, 256:256 + TILES]).then_inc(step("tok_set"), 1)
            for v, slot in ((slots[:, 0:NT], slot_a), (slots[:, NT:], slot_b)):
                dve.tensor_copy(slot, v).then_inc(sem("slot_ready"), 1)
            for v, wgt in ((s1, wgt_a), (s2, wgt_b)):
                link(dve.tensor_tensor(three(hit), three(sl), b3(v, NE), ALU.is_equal))
                link(dve.tensor_tensor(hit, hit, comb, ALU.mult))
                dve.tensor_reduce(wgt, three(hit), AX_X, ALU.add).then_inc(sem("weights_set"), 1)
                dve.wait_ge(sem("weights_set"), 1 if wgt is wgt_a else 2)

            def take_rows(t, j):
                dve.wait_ge(sem("moe_T"), t + 1)
                if not (isinstance(t, int) and t < 2):
                    dve.wait_ge(sem("moe_gu"), t - 1)
                dve.tensor_copy(rowT[j % 2][:, 4:8], bank(3).rearrange("p (k t) -> p k t", t=P)).then_inc(sem("rowT_dve"), 1)

            def take_answer(t, j, r):
                dve.wait_ge(sem("moe_dn"), t + 1)
                if not (isinstance(t, int) and t < 2):
                    dve.wait_ge(sem(f"y_out{j % 2}"), 32 * r + 16 * (j // 2))
                dve.tensor_tensor(answer[j % 2], bank(5, 2), gfb, ALU.mult).then_inc(sem("y_taken"), 1)

            def hidden(t, j, r):
                dve.wait_ge(sem("silu_ready"), t + 1)
                if not (isinstance(t, int) and t < 2):
                    dve.wait_ge(sem("moe_HT"), t - 1)
                dve.tensor_tensor(hid[j % 2], silu[j % 2], bank(j % 2)[:, FF:2 * FF], ALU.mult).then_inc(sem("hid_ready"), 1)
                if not (isinstance(t, int) and t == 0):
                    take_answer(t - 1, (j - 1) % 4, r if j else r - 1)
                if not (isinstance(t, int) and t == TILES - 1):
                    take_rows(t + 1, (j + 1) % 4)
                dve.wait_ge(sem("moe_HT"), t + 1)
                if not (isinstance(t, int) and t < 2):
                    dve.wait_ge(sem("moe_dn"), t - 1)
                dve.tensor_copy(hidT[j % 2], bank(4)[:, 0:FF].rearrange("p (k t) -> p k t", t=P)).then_inc(sem("hidT_ready"), 1)

            dve.wait_ge(sem("last_in"), 32)
            take_rows(0, 0)
            each_tile(dve, hidden)
            take_answer(TILES - 1, (TILES - 1) % 4, TILES // 4)

            for i in range(NT + 1):
                if i < NT:
                    b = i % NY
                    dve.wait_ge(sem(f"ya_in{b}"), 16 * (i // NY + 1))
                    link(dve.scalar_tensor_tensor(out=x2[:, i], in0=y_a[b], scalar=wgt_a[:, i:i + 1], in1=x2[:, i], op0=ALU.mult, op1=ALU.add))
                    dve.wait_ge(sem(f"yb_in{b}"), 16 * (i // NY + 1))
                    dve.scalar_tensor_tensor(out=x2[:, i], in0=y_b[b], scalar=wgt_b[:, i:i + 1], in1=x2[:, i], op0=ALU.mult, op1=ALU.add).then_inc(sem("x3_ready"), 1)
                if i >= 1:
                    c = i - 1
                    dve.wait_ge(sem("rstd3"), c + 1)
                    if c >= 2:
                        dve.wait_ge(sem(f"out{c % 2}"), 16 * (c // 2))
                    dve.scalar_tensor_tensor(out=fin[c % 2], in0=x2[:, c], scalar=rstd3[:, c:c + 1], in1=fnw, op0=ALU.mult, op1=ALU.mult).then_inc(sem("fin_ready"), 1)

        @block.tensor
        def _(pe):
            def modulation(n):
                pe.wait_ge(sem(f"ada_in{n % 2}"), 16 * (n // 2 + 1))
                if n >= 4:
                    pe.wait_ge(sem("mod_row"), n - 3)
                for k in range(KD):
                    mm = pe.matmul(bank(n % 4)[0:1], cact[:, k:k + 1], ada_ring[n % 2][:, k], start=(k == 0), stop=(k == KD - 1))
                mm.then_inc(sem("ada_mm"), 1)

            pe.wait_ge(step("cact"), nth("cact"))
            modulation(0)
            modulation(1)
            pe.wait_ge(sem("const_in"), 32)
            modulation(2)
            modulation(3)
            modulation(4)
            modulation(5)
            pe.wait_ge(step("s5_BA"), nth("s5_BA"))
            pe.wait_ge(step("s5_CA"), nth("s5_CA"))
            for m in range(S5_M):
                for a in range(2):
                    mm = pe.transpose(psum[:, 2048 + (2 * m + a) * P:2048 + (2 * m + a + 1) * P],
                                      s5_BA[:, a, m].rearrange("p s c -> p (s c)"), ident)
            mm.then_inc(step("s5_W_tr"), 1)
            pe.wait_ge(sem("s5_W"), 4)
            for par in range(2):
                h = slice(64 * par, 64 * par + 64)
                for m in range(S5_M):
                    o = psum[0:S5_C, 2048 + 1024 * par + m * P:2048 + 1024 * par + (m + 1) * P]
                    for a in range(2):
                        mm = pe.matmul(o, s5_bb[h, a, m], s5_CA[h, a, m, 0:8].rearrange("p n c -> p (n c)"),
                                       start=(a == 0), stop=(a == 1))
            mm.then_inc(step("s5_kern"), 1)
            for n in range(6, 12):
                modulation(n)
            pe.wait_ge(step("kz_full"), nth("kz_full"))
            for i in range(NT):
                pe.wait_ge(sem("h_add"), i + 1)
                if i >= 2:
                    pe.wait_ge(sem("hT_act"), i - 1)
                    pe.wait_ge(sem("hT_dve"), i - 1)
                for k in range(KD):
                    mm = pe.transpose(psum[:, 2048 + 1024 * (i % 2) + k * P:2048 + 1024 * (i % 2) + (k + 1) * P],
                                      x_sb[:, i, k * P:(k + 1) * P], ident)
                mm.then_inc(sem("h_tr"), 1)

            def project(name):
                for u in unit_range(name):
                    g, where = UNITS[u]
                    _, _, w, tok, _ = GROUPS[g]
                    ring = win_ring[g % 2]
                    if u == unit_range(name)[0]:
                        pe.wait_ge(sem(f"win_in{g % 2}"), 16 * (g // 2 + 1))
                    if u >= WIN_BANKS:
                        for e in ("act", "dve"):
                            if evacuated(e, u - WIN_BANKS):
                                pe.wait_ge(sem(f"ev_{e}"), evacuated(e, u - WIN_BANKS))
                    for k in range(KD):
                        if name == "su":
                            mm = pe.matmul(bank(u % WIN_BANKS)[:, 0:w], hT[:, k, where::S5_L], ring[:, k, 0:w], start=(k == 0), stop=(k == KD - 1))
                        elif tok:
                            mm = pe.matmul(bank(u % WIN_BANKS)[:, 0:w], hT[:, k, where * P:(where + 1) * P], ring[:, k, 0:w],
                                           start=(k == 0), stop=(k == KD - 1))
                        else:
                            m, h = where
                            mm = pe.matmul(bank(u % WIN_BANKS), ring[:, k, m * P:(m + 1) * P], hT[:, k, 512 * h:512 * h + 512],
                                           start=(k == 0), stop=(k == KD - 1))
                    mm.then_inc(sem("win_mm"), 1)

            pe.wait_ge(sem("hT_act"), NT)
            pe.wait_ge(sem("hT_dve"), NT)
            pe.wait_ge(sem("mod_row"), 12)
            project("su")
            pe.wait_ge(sem("ev_dve"), evacuated("dve", NT - 1))
            for g in range(S5_G):
                mm = pe.transpose(psum[:, 2048 + g * P:2048 + (g + 1) * P], s5_Z[:, g].rearrange("p s c -> p (s c)"), ident)
            mm.then_inc(step("s5_U_tr"), 1)
            project("hq")
            pe.wait_ge(sem("s5_U"), 4)
            for a in range(2):
                for g in range(S5_G):
                    m, h = g // 2, 64 * (g % 2)
                    mm = pe.matmul(psum[h:h + 64, 2048 + 1024 * a + m * P:2048 + 1024 * a + (m + 1) * P],
                                   s5_W[:, m, a, h:h + 64], s5_U[:, g], start=True, stop=True)
            mm.then_inc(step("s5_V_mm"), 1)
            project("hi")
            project("hg")
            pe.wait_ge(sem("s5_X"), 2)
            pe.wait_ge(sem("s5_T_in"), 16 * S5_L)
            for par in range(2):
                h = slice(64 * par, 64 * par + 64)
                for m in range(S5_M):
                    o = psum[:, 2048 + 1024 * par + m * P:2048 + 1024 * par + (m + 1) * P]
                    pe.matmul(o, s5_U[:, 2 * m + par], s5_T[:, 2 * m + par], start=True, stop=False)
                    for a in range(2):
                        mm = pe.matmul(o, s5_X[a][h, m], s5_CA[h, a, m, 1:9].rearrange("p n c -> p (n c)"), start=False, stop=(a == 1))
            mm.then_inc(step("s5_y_mm"), 1)
            project("hf")
            pe.wait_ge(sem("s5_gelu"), 4)
            for c in range(2):
                for st in range(S5_L):
                    mm = pe.transpose(psum[:, 2048 + (8 * c + st) * P:2048 + (8 * c + st + 1) * P], s5_y[:, st, c * P:(c + 1) * P], ident)
            mm.then_inc(step("s5_y_tr"), 1)
            project("fv")
            pe.wait_ge(sem("s5_yT"), 4)
            pe.wait_ge(sem("glu_in"), 16)
            for st in range(S5_L):
                o = psum[:, 2048 + S5_W * st:2048 + S5_W * (st + 1)]
                pe.matmul(o, ones[0:1], glu_b, start=True, stop=False)
                for c in range(2):
                    mm = pe.matmul(o, s5_yT[:, c, st], glu_w[:, c], start=False, stop=(c == 1))
            mm.then_inc(step("s5_glu_mm"), 1)
            project("fq")
            pe.wait_ge(step("s5_o"), nth("s5_o"))
            for c in range(2):
                for st in range(S5_L):
                    mm = pe.transpose(psum[:, 2048 + (8 * c + st) * P:2048 + (8 * c + st + 1) * P], s5_y[:, st, c * P:(c + 1) * P], ident)
            mm.then_inc(step("s5_o_tr"), 1)
            project("fk")

            def keep_clock(n):
                for _ in range(n):
                    pe.matmul(bank(7), ident16[:], idle16, start=True, stop=True)

            def level_scores(rnd, l):
                for u in range(HG_H):
                    c = (rnd * (1 + n_lev) + l) * HG_H + u
                    if c >= 4:
                        pe.wait_ge(sem("hg_taken"), c - 3)
                    if l == 0:
                        hs, m = slice(64 * (u % 2), 64 * (u % 2) + 64), u // 2
                        for n in range(4):
                            ts = slice((4 * rnd + n) * P, (4 * rnd + n + 1) * P)
                            mm = pe.matmul(bank(c % 4)[:, n * P:(n + 1) * P], hk[hs, m, ts], hq[hs, m, ts], start=True, stop=True)
                    else:
                        m, b = u // 2, (rnd * n_lev + l - 1) % 2
                        for n in range(2):
                            ts = slice((2 * (u % 2) + n) * P, (2 * (u % 2) + n + 1) * P)
                            mm = pe.matmul(bank(c % 4)[:, 2 * n * P:2 * (n + 1) * P].rearrange("p (g t) -> p g t", g=2),
                                           lev[b][:, m, ts], lev_q[b][m][:, :, ts], start=True, stop=True)
                    mm.then_inc(sem("hg_mm"), 1)

            pe.wait_ge(sem("ev_dve"), evacuated("dve", len(UNITS) - 1))
            pe.wait_ge(sem("ev_act"), evacuated("act", len(UNITS) - 1))
            pe.wait_ge(sem("s5_done"), 4)
            pe.wait_ge(step("hk_ready"), nth("hk_ready"))
            for rnd in range(2):
                level_scores(rnd, 0)
                if rnd == 0:
                    pe.wait_ge(sem("flog"), 2)
                    for i in range(NT):
                        mm = pe.transpose(psum[0:FOX_H, 2048 + i * P:2048 + (i + 1) * P], flog[:, i * FOX_H:(i + 1) * FOX_H], ident)
                    mm.then_inc(step("f_tr"), 1)
                    pe.wait_ge(step("cum_ready"), nth("cum_ready"))
                    pe.wait_ge(step("ke_ready"), nth("ke_ready"))
                    for n in range(NT):
                        if n >= 4:
                            pe.wait_ge(sem("keT_ready"), n - 3)
                        for m in range(HG_M):
                            mm = pe.transpose(bank(4 + n % 4)[:, m * P:(m + 1) * P], ke[:, m, n * P:(n + 1) * P], ident)
                        mm.then_inc(sem("ke_tr"), 1)
                    pe.wait_ge(sem("keT_ready"), NT)
                    for n in range(NT - 1):
                        for h in range(HG_H):
                            p0, o = 64 * (h % 2), 2048 + 512 * (n // 2) + 192 * (n % 2) + 64 * (h // 2)
                            mm = pe.matmul(psum[p0:p0 + 64, o:o + 64], keT[n][:, 64 * h:64 * h + 64], hv[:, n, 64 * h:64 * h + 64], start=True, stop=True)
                        mm.then_inc(sem("dS_mm"), 1)
                    pe.wait_ge(sem("mask16"), 2)
                    pe.wait_ge(sem("hg_S"), NT - 1)
                    keep_clock(16)
                for l in range(1, 1 + n_lev):
                    pe.wait_ge(sem("lev_q"), rnd * n_lev + l)
                    pe.wait_ge(sem("lev_k"), rnd * n_lev + l)
                    level_scores(rnd, l)
                pe.wait_ge(sem("hg_taken"), (rnd + 1) * (1 + n_lev) * HG_H)
                if rnd:
                    pe.wait_ge(sem("hg_o_taken"), 4)
                pe.wait_ge(step("qe_ready"), nth("qe_ready"))
                for h in [0, 2, 4, 1, 3, 5]:
                    hs, m = slice(64 * (h % 2), 64 * (h % 2) + 64), h // 2
                    for n in range(4):
                        o0 = 2048 + 1024 * (h % 2) + 512 * (n // 2) + 192 * (n % 2) + 64 * m
                        first = 4 * rnd + n == 0
                        mm = pe.matmul(psum[:, o0:o0 + 64], sT[:, h, n], hv[:, 4 * rnd + n, 64 * h:64 * h + 64], start=True, stop=first)
                        if not first:
                            mm = pe.matmul(psum[:, o0:o0 + 64], qe[hs, m, (4 * rnd + n) * P:(4 * rnd + n + 1) * P],
                                           hg_S[hs, 4 * rnd + n - 1, 64 * m:64 * m + 64], start=False, stop=True)
                mm.then_inc(sem("hg_o_mm"), 1)
            for n in range(NT):
                pe.wait_ge(sem("hg_gated"), n // 4 + 1)
                pe.wait_ge(sem("hg_o_taken"), 8)
                if n >= 4:
                    pe.wait_ge(sem("cHg_ready"), n - 3)
                for m in range(HG_M):
                    mm = pe.transpose(bank(4 + n % 4)[:, m * P:(m + 1) * P], hgate[:, n, m * P:(m + 1) * P], ident)
                mm.then_inc(sem("hg_o_tr"), 1)

            pe.wait_ge(sem("cHg_ready"), NT)
            keep_clock(8)
            pe.wait_ge(sem("aug_in"), 16 * 2 * FOX_H)

            def logits(u):
                i, h = units[u]
                if u >= 2:
                    pe.wait_ge(sem("f_exp"), u - 1)
                w = (i + 1) * P
                s0 = 1024 * (u % 2)
                for c in range(0, w, 512):
                    e = min(w, c + 512)
                    mm = pe.matmul(psum[:, s0 + c:s0 + e], qaug[:, h, i * P:(i + 1) * P], kaug[:, h, c:e], start=True, stop=(e < w))
                pe.matmul(psum[:, s0 + w - P:s0 + w], ident16[:], neg16[:], start=False, stop=True).then_inc(sem("f_qk"), 1)

            def turn(u):
                i, h = units[u]
                pe.wait_ge(sem("f_exp"), u + 1)
                if u >= 1:
                    pe.wait_ge(sem("fT_dve"), u)
                    pe.wait_ge(sem("fT_act"), sum(units[v][0] >= 4 for v in range(u))) if units[u - 1][0] >= 4 else None
                for kb in range(i + 1):
                    mm = pe.transpose(psum[:, 2048 + kb * P:2048 + (kb + 1) * P], prob[u % 2][:, kb * P:(kb + 1) * P], ident)
                mm.then_inc(sem("f_T"), 1)

            def values(u):
                i, h = units[u]
                pe.wait_ge(sem("fT_dve"), u + 1)
                if i >= 4:
                    pe.wait_ge(sem("fT_act"), sum(units[v][0] >= 4 for v in range(u + 1)))
                if h == 0 and i >= 2:
                    pe.wait_ge(sem("cFox_ready"), i - 1)
                for kb in range(i + 1):
                    mm = pe.matmul(bank(6 + i % 2)[:, h * FOX_D:(h + 1) * FOX_D], probT[u % 2][:, kb], fv[:, kb, h * FOX_D:(h + 1) * FOX_D],
                                   start=(kb == 0), stop=(kb == i))
                mm.then_inc(sem("f_pv"), 1)

            def fox_out(i):
                pe.wait_ge(sem("fo_ready"), i + 1)
                for m in range(3):
                    mm = pe.transpose(bank(6 + i % 2)[:, m * P:(m + 1) * P], fo[i % 2][:, m * P:(m + 1) * P], ident)
                mm.then_inc(sem("fo_tr"), 1)

            logits(0)
            for u in range(len(units)):
                if u + 1 < len(units):
                    logits(u + 1)
                turn(u)
                if u >= 1:
                    values(u - 1)
                i, h = units[u]
                if i >= 1 and h == 4:
                    fox_out(i - 1)
            values(len(units) - 1)
            fox_out(NT - 1)

            pe.wait_ge(sem("cFox_ready"), NT)
            pe.wait_ge(step("w_scaled"), nth("w_scaled"))

            def mix(i):
                if i >= 2:
                    pe.wait_ge(sem("mix_taken"), i - 1)
                for n in range(2):
                    for k in range(KD):
                        mm = pe.matmul(bank(2 * (i % 2) + n), branch[k][:, i * P:(i + 1) * P], w_out[:, k, 512 * n:512 * n + 512],
                                       start=(k == 0), stop=(k == KD - 1))
                mm.then_inc(sem("mix_mm"), 1)

            def turn_h2(i):
                pe.wait_ge(sem("h2_ready"), i + 1)
                if i >= 1:
                    pe.wait_ge(sem("h2T_act"), i)
                    pe.wait_ge(sem("h2T_dve"), i)
                for k in range(KD):
                    mm = pe.transpose(psum[:, 2048 + k * P:2048 + (k + 1) * P], h2[i % 2][:, k * P:(k + 1) * P], ident)
                mm.then_inc(sem("h2_tr"), 1)

            def route(i):
                pe.wait_ge(sem("h2T_act"), i + 1)
                pe.wait_ge(sem("h2T_dve"), i + 1)
                o = bank(6)[:, NE * i:NE * (i + 1)]
                pe.matmul(o, ones[0:1], router_b, start=True, stop=False)
                for k in range(KD):
                    mm = pe.matmul(o, h2T[i % 2][:, k], router_w[:, k], start=False, stop=(k == KD - 1))
                mm.then_inc(sem("route_mm"), 1)

            mix(0)
            for i in range(NT):
                if i + 1 < NT:
                    mix(i + 1)
                turn_h2(i)
                if i >= 1:
                    route(i - 1)
            route(NT - 1)
            pe.wait_ge(step("chosen"), nth("chosen"))
            pe.matmul(bank(7)[:, 0:P], cst[:, C_LT:C_LT + P], rt[5], start=True, stop=True)
            pe.matmul(bank(7)[:, P:2 * P], ones, rt[5], start=True, stop=True).then_inc(step("count_mm"), 1)
            pe.wait_ge(sem("numbered"), 2)
            pe.wait_ge(step("picks"), nth("picks"))
            for n in range(2 * NT):
                mm = pe.matmul(bank(7)[:, 256:288], place[:, n], number[:, n], start=(n == 0), stop=(n == 2 * NT - 1))
            mm.then_inc(step("list_mm"), 1)

            def turn_rows(t, j, r):
                pe.wait_ge(sem(f"row_in{j}"), 16 * r + 16)
                for k in range(KD):
                    mm = pe.transpose(psum[:, 1024 + k * P:1024 + (k + 1) * P], rows[j][:, k * P:(k + 1) * P], ident)
                mm.then_inc(sem("moe_T"), 1)

            def down(t, j, r):
                pe.wait_ge(sem("hidT_ready"), t + 1)
                pe.wait_ge(sem(f"dn_in{j}"), 16 * r + 16)
                if not (isinstance(t, int) and t == 0):
                    pe.wait_ge(sem("y_taken"), t)
                for n in range(2):
                    for k in range(2):
                        mm = pe.matmul(bank(5 + n), hidT[j % 2][:, k], wdn[j][:, k, 512 * n:512 * n + 512], start=(k == 0), stop=(k == 1))
                mm.then_inc(sem("moe_dn"), 1)

            def expert(t, j, r):
                pe.wait_ge(sem("rowT_act"), t + 1)
                pe.wait_ge(sem("rowT_dve"), t + 1)
                if not (isinstance(t, int) and t < 2):
                    pe.wait_ge(sem("hid_ready"), t - 1)
                pe.wait_ge(sem(f"gu_in{j}"), 16 * r + 16)
                for k in range(KD):
                    mm = pe.matmul(bank(j % 2), rowT[j % 2][:, k], wgu[j][:, k], start=(k == 0), stop=(k == KD - 1))
                mm.then_inc(sem("moe_gu"), 1)
                if not (isinstance(t, int) and t == 0):
                    down(t - 1, (j - 1) % 4, r if j else r - 1)
                if not (isinstance(t, int) and t == TILES - 1):
                    turn_rows(t + 1, (j + 1) % 4, r if j < 3 else r + 1)
                pe.wait_ge(sem("hid_ready"), t + 1)
                if not (isinstance(t, int) and t == 0):
                    pe.wait_ge(sem("hidT_ready"), t)
                for k in range(2):
                    mm = pe.transpose(bank(4)[:, k * P:(k + 1) * P], hid[j % 2][:, k * P:(k + 1) * P], ident)
                mm.then_inc(sem("moe_HT"), 1)

            turn_rows(0, 0, 0)
            each_tile(pe, expert)
            down(TILES - 1, (TILES - 1) % 4, TILES // 4)


def lay_out(a):
    def pairs(v):
        v = v.reshape(S5_M, 2, S5_P, -1).transpose(1, 2, 0, 3)
        return v.reshape(P, -1)

    def blocks(v):
        return v.reshape(-1, P, v.size // v.shape[0]).transpose(1, 0, 2).reshape(P, -1)

    rows = lambda v: np.broadcast_to(v.reshape(1, -1), (P, v.size))
    d = np.zeros((P, S5_G), np.float32)
    d[0:S5_C] = a["s5_d"][0].T
    dt = np.broadcast_to(a["s5_log_dt"][0][:, None], (S5_G, S5_P))
    w = {n: a[n] for n in ("x", "ada_b")}
    w["ada_w"] = a["ada_w"][0].reshape(KD, P, ADA // ADA_N, ADA_N).transpose(2, 1, 0, 3)
    w["w_in"] = a["w_in"][0].reshape(KD, P, N_IN).transpose(1, 0, 2)
    w["c_col"] = blocks(a["c"][0])
    w["s5_par"] = np.concatenate([pairs(a["s5_a_re"][0]), pairs(a["s5_a_im"][0]), pairs(dt), d,
                                  pairs(a["s5_b_re"][0]), pairs(a["s5_b_im"][0]),
                                  pairs(a["s5_c_re"][0].transpose(0, 2, 1)), pairs(a["s5_c_im"][0].transpose(0, 2, 1))], 1)
    w["late"] = np.concatenate([rows(a["fox_f_bias"][0]),
                                blocks(np.concatenate([a["branch_norm_fox"][0], a["branch_norm_s5"][0],
                                                       np.tile(a["hgrn_norm_w"][0], HG_H)])),
                                blocks(a["router_w"]), rows(a["router_b"])], 1)
    w["glu"] = np.concatenate([blocks(a["s5_glu_w"][0]), rows(a["s5_glu_b"][0])], 1)
    w["w_out"] = blocks(a["w_out"][0])
    w["norms"] = np.concatenate([a["norm_mix_w"], a["norm_ffn_w"], a["final_norm_w"][None]])
    w["gate_up"] = np.concatenate([a["moe_w_gate"][0], a["moe_w_up"][0]], 2).reshape(NE, KD, P, 2 * FF).transpose(0, 2, 1, 3)
    w["down"] = a["moe_w_down"][0].reshape(NE, 2, P, D).transpose(0, 2, 1, 3)
    w["cst"], w["lmask"] = shape_constants()
    return {f"in_{n}": np.ascontiguousarray(v) for n, v in w.items()}


def kernel(**inputs):
    import concourse.bacc as _bacc
    from concourse.bass_utils import run_bass_kernel_spmd as _run

    nc = _bacc.Bacc("TRN2", target_bir_lowering=False, num_devices=1)
    arrays = lay_out(inputs)
    A = {n[3:]: nc.dram_tensor(n, a.shape, mybir.dt.from_np(a.dtype), kind="ExternalInput").ap() for n, a in arrays.items()}
    out = nc.dram_tensor("out", (1, T, D), F32, kind="ExternalOutput").ap()
    hybrid_trunk_layer(nc, A, out)
    r = _run(nc, [arrays], core_ids=[0])
    return r.results[0]["out"]
```
